# Optimizing a Trainium2 kernel written in Bass

```python
import math
import jax, jax.numpy as jnp
from jax import lax
import numpy as np

D_MODEL = 2048
BATCH = 1
SEQ = 256
DEPTH = 2

HEAD_DIM = 128
A_WIDTH = D_MODEL // 2
A_GROUPS = A_WIDTH // 128
CHUNK = 128
B_HEADS = (D_MODEL // 2) // HEAD_DIM
B_WIDTH = B_HEADS * HEAD_DIM
DILATED_PAIRS = ((128, 1), (512, 4), (2048, 16))
ATT_BLOCK = 128
C_HEADS = D_MODEL // HEAD_DIM
C_WIDTH = C_HEADS * HEAD_DIM
D_FF = 4 * D_MODEL
N_EVEN = (DEPTH + 1) // 2
N_ODD = DEPTH // 2
RMS_EPS = 1e-6
LN_EPS = 1e-5

kernel_name = "hybrid_gmlp_dilated_stickbreak_trunk"

def rmsnorm(x, g):
    xf = x.astype(jnp.float32)
    y = xf * lax.rsqrt(jnp.mean(xf * xf, axis=-1, keepdims=True) + RMS_EPS)
    return (y * g.astype(jnp.float32)).astype(x.dtype)

def layernorm(x, g, b):
    xf = x.astype(jnp.float32)
    mu = jnp.mean(xf, axis=-1, keepdims=True)
    var = jnp.mean(jnp.square(xf - mu), axis=-1, keepdims=True)
    y = (xf - mu) * lax.rsqrt(var + LN_EPS)
    return (y * g.astype(jnp.float32) + b.astype(jnp.float32)).astype(x.dtype)

def alibi_slopes(n):
    return jnp.exp2(-8.0 * (jnp.arange(n, dtype=jnp.float32) + 1.0) / n)

def spatial_gating_unit(u, v, ln_g, ln_b, w_s, b_s):
    bsz, t, _ = v.shape
    v = layernorm(v, ln_g, ln_b)
    vg = v.reshape(bsz, t // CHUNK, CHUNK, A_GROUPS, A_WIDTH // A_GROUPS)
    w = jnp.tril(w_s).astype(v.dtype)
    mixed = jnp.einsum('gij,bcjgd->bcigd', w, vg) + b_s.T.astype(v.dtype)[None, None, :, :, None]
    return u * mixed.reshape(bsz, t, A_WIDTH)

def dilated_branch(q, k, v, window, dilation, slopes):
    bsz, t, h, dh = q.shape
    blk = ATT_BLOCK
    win_sub = window // dilation
    period = dilation * blk
    tp = -(-t // period) * period
    pad = tp - t
    sub_len = tp // dilation
    nb = sub_len // blk

    def to_sub(a):
        a = jnp.pad(a, ((0, 0), (0, pad), (0, 0), (0, 0)))
        a = a.reshape(bsz, sub_len, dilation, h, dh).transpose(0, 2, 3, 1, 4)
        return a.reshape(bsz, dilation, h, nb, blk, dh)

    qs, ks, vs = to_sub(q), to_sub(k), to_sub(v)

    def with_prev(a):
        prev = jnp.concatenate([jnp.zeros_like(a[:, :, :, :1]), a[:, :, :, :-1]], axis=3)
        return jnp.concatenate([prev, a], axis=4)

    kw, vw = with_prev(ks), with_prev(vs)
    s = jnp.einsum('brhnqe,brhnke->brhnqk', qs, kw).astype(jnp.float32)

    qi = jnp.arange(blk)[:, None]
    kj = jnp.arange(2 * blk)[None, :]
    dist = qi + blk - kj
    band = (dist >= 0) & (dist <= win_sub)
    first = (jnp.arange(nb) == 0)[:, None, None] & (kj < blk)[None]
    valid = band[None] & ~first
    bias = -slopes[:, None, None] * (dist * dilation).astype(jnp.float32)[None]
    s = s + bias[None, None, :, None]
    s = jnp.where(valid[None, None, None], s, -jnp.inf)
    m = jnp.max(s, axis=-1, keepdims=True)
    p = jnp.exp(s - m)
    den = jnp.sum(p, axis=-1, keepdims=True)
    o = jnp.einsum('brhnqk,brhnke->brhnqe', p, vw.astype(jnp.float32)) / den
    lse = (m + jnp.log(den))[..., 0]

    o = o.reshape(bsz, dilation, h, sub_len, dh).transpose(0, 3, 1, 2, 4).reshape(bsz, tp, h, dh)[:, :t]
    lse = lse.reshape(bsz, dilation, h, sub_len).transpose(0, 3, 1, 2).reshape(bsz, tp, h)[:, :t]
    return o, lse

def dilated_mixture(q, k, v):
    slopes = alibi_slopes(q.shape[2])
    outs, lses = [], []
    for window, dilation in DILATED_PAIRS:
        o, lse = dilated_branch(q, k, v, window, dilation, slopes)
        outs.append(o)
        lses.append(lse)
    wts = jax.nn.softmax(jnp.stack(lses, axis=0), axis=0)
    o = jnp.sum(wts[..., None] * jnp.stack(outs, axis=0), axis=0)
    return o.astype(q.dtype)

def gmlp_dilated_layer(h, w_in, ln_g, ln_b, w_s, b_s, w_out):
    bsz, t, _ = h.shape
    z = h @ w_in
    u, va, q, k, vb = jnp.split(z, [A_WIDTH, 2 * A_WIDTH, 2 * A_WIDTH + B_WIDTH, 2 * A_WIDTH + 2 * B_WIDTH], axis=-1)
    a_out = spatial_gating_unit(jax.nn.gelu(u, approximate=False), jax.nn.gelu(va, approximate=False), ln_g, ln_b, w_s, b_s)
    q = q.reshape(bsz, t, B_HEADS, HEAD_DIM) * (HEAD_DIM ** -0.5)
    k = k.reshape(bsz, t, B_HEADS, HEAD_DIM)
    vb = vb.reshape(bsz, t, B_HEADS, HEAD_DIM)
    b_out = dilated_mixture(q, k, vb).reshape(bsz, t, B_WIDTH)
    return jnp.concatenate([a_out, b_out], axis=-1) @ w_out

def stick_breaking_attention(q, k, v):
    bsz, h, t, dh = q.shape
    nb = t // ATT_BLOCK
    qb = q.reshape(bsz, h, nb, ATT_BLOCK, dh).transpose(2, 0, 1, 3, 4)
    kpos = jnp.arange(t)

    def block(args):
        qblk, start = args
        z = jnp.einsum('bhqe,bhke->bhqk', qblk, k).astype(jnp.float32)
        qpos = start + jnp.arange(ATT_BLOCK)
        causal = kpos[None, :] < qpos[:, None]
        log_1m_beta = jnp.where(causal, jax.nn.log_sigmoid(-z), 0.0)
        rev = lax.cumsum(log_1m_beta, axis=3, reverse=True)
        excl = jnp.concatenate([rev[..., 1:], jnp.zeros_like(rev[..., :1])], axis=-1)
        a = jnp.where(causal, jnp.exp(jax.nn.log_sigmoid(z) + excl), 0.0)
        return jnp.einsum('bhqk,bhke->bhqe', a.astype(v.dtype), v)

    o = lax.map(block, (qb, jnp.arange(nb) * ATT_BLOCK))
    return o.transpose(1, 0, 3, 2, 4).reshape(bsz, t, h * dh)

def stick_breaking_layer(h, w_in, w_out):
    bsz, t, _ = h.shape
    q, k, v = jnp.split(h @ w_in, 3, axis=-1)
    def heads(a):
        return a.reshape(bsz, t, C_HEADS, HEAD_DIM).transpose(0, 2, 1, 3)
    o = stick_breaking_attention(heads(q) * (HEAD_DIM ** -0.5), heads(k), heads(v))
    return o @ w_out

def squared_relu_mlp(h, w1, w2):
    return jnp.square(jax.nn.relu(h @ w1)) @ w2

def setup_inputs(seed: int = 0) -> dict:
    key = jax.random.key(seed)
    ks = jax.random.split(key, 16)
    f32 = jnp.float32
    def nrm(k, shape, scale):
        return jax.random.normal(k, shape, f32) * scale
    def gain(k, shape):
        return 1.0 + 0.02 * jax.random.normal(k, shape, f32)
    return {
        "x": jax.random.normal(ks[0], (BATCH, SEQ, D_MODEL), f32),
        "norm_pre_mix": gain(ks[1], (DEPTH, D_MODEL)),
        "norm_post_mix": gain(ks[2], (DEPTH, D_MODEL)),
        "norm_pre_ffn": gain(ks[3], (DEPTH, D_MODEL)),
        "norm_post_ffn": gain(ks[4], (DEPTH, D_MODEL)),
        "ab_w_in": nrm(ks[5], (N_EVEN, D_MODEL, 2 * A_WIDTH + 3 * B_WIDTH), D_MODEL ** -0.5),
        "sgu_ln_g": gain(ks[6], (N_EVEN, A_WIDTH)),
        "sgu_ln_b": nrm(ks[7], (N_EVEN, A_WIDTH), 0.02),
        "sgu_w": nrm(ks[8], (N_EVEN, A_GROUPS, CHUNK, CHUNK), CHUNK ** -0.5),
        "sgu_b": 1.0 + nrm(ks[9], (N_EVEN, A_GROUPS, CHUNK), 0.1),
        "ab_w_out": nrm(ks[10], (N_EVEN, A_WIDTH + B_WIDTH, D_MODEL), (A_WIDTH + B_WIDTH) ** -0.5),
        "sb_w_in": nrm(ks[11], (N_ODD, D_MODEL, 3 * C_WIDTH), D_MODEL ** -0.5),
        "sb_w_out": nrm(ks[12], (N_ODD, C_WIDTH, D_MODEL), C_WIDTH ** -0.5),
        "ffn_w1": nrm(ks[13], (DEPTH, D_MODEL, D_FF), D_MODEL ** -0.5),
        "ffn_w2": nrm(ks[14], (DEPTH, D_FF, D_MODEL), D_FF ** -0.5),
    }

def reference(x, norm_pre_mix, norm_post_mix, norm_pre_ffn, norm_post_ffn,
              ab_w_in, sgu_ln_g, sgu_ln_b, sgu_w, sgu_b, ab_w_out,
              sb_w_in, sb_w_out, ffn_w1, ffn_w2):
    for layer in range(DEPTH):
        h = rmsnorm(x, norm_pre_mix[layer])
        i = layer // 2
        if layer % 2 == 0:
            y = gmlp_dilated_layer(h, ab_w_in[i], sgu_ln_g[i], sgu_ln_b[i], sgu_w[i], sgu_b[i], ab_w_out[i])
        else:
            y = stick_breaking_layer(h, sb_w_in[i], sb_w_out[i])
        x = x + rmsnorm(y, norm_post_mix[layer])
        h = rmsnorm(x, norm_pre_ffn[layer])
        y = squared_relu_mlp(h, ffn_w1[layer], ffn_w2[layer])
        x = x + rmsnorm(y, norm_post_ffn[layer])
    return x


_drawn_inputs = setup_inputs


def setup_inputs(seed=0):
    import zlib

    import numpy as np

    out = dict(_drawn_inputs(seed))
    spreads = {}
    factors = {'norm_post_mix': 2.941,
     'norm_pre_ffn': 3.245,
     'norm_post_ffn': 10.363,
     'sgu_ln_g': 6.931,
     'sgu_ln_b': 7.124}
    for name, (base, spread) in spreads.items():
        noise = np.random.default_rng([zlib.crc32(name.encode()), seed]).standard_normal(out[name].shape)
        drawn = base * np.exp(spread * noise) if base else spread * noise
        out[name] = __import__('jax').numpy.asarray(drawn.astype(out[name].dtype))
    for name, factor in factors.items():
        out[name] = (out[name] * factor).astype(out[name].dtype)
    return out
```

```python
from contextlib import ExitStack

import numpy as np

import concourse.bass as bass
from concourse import mybir

F32 = mybir.dt.float32
F32R = mybir.dt.float32r
ALU = mybir.AluOpType
ACT = mybir.ActivationFunctionType
AX = mybir.AxisListType

P = 128
T = 256
TB = T // P
D = 2048
KT = D // P
NC = 512
TICKS = KT // 2
QUARTERS = 4
RING = 4
A_W = D // 2
GROUPS = A_W // P
LAYERS = 2
DFF = 4 * D
FGROUPS = DFF // D
HG = 4
L0_HEADS = 8
L1_GROUPS = 4
SCALE = float(P) ** -0.5
RMS_EPS = 1e-6
LN_EPS = 1e-5
TRI = 3 * P
FAR = 1e30

U_IN0, U_OUT0, U_FFN0, U_IN1, U_OUT1, U_FFN1, UNITS = 0, 10, 14, 46, 58, 62, 94
OUT_ORDER = ([(u, s) for u in range(3) for s in range(6)] + [(u, s) for u in range(3) for s in (6, 7)]
             + [(3, s) for s in range(8)])
OUT_BUF = [0, 1, 2, 0]
OUT_POST = {20: 0, 22: 1, 24: 2}


def shape_constants():
    p = np.arange(P)[:, None]
    j = np.arange(P)[None, :]
    dist = np.concatenate([p - j, p + P - j, p - j], axis=1)
    causal = dist >= 0
    count = (causal & (dist <= 128)).astype(np.float32) + (causal & (dist % 4 == 0)) + (causal & (dist % 16 == 0))
    far = np.where(count > 0, dist, FAR)
    strict = p < j
    keep = np.concatenate([strict, np.ones((P, P), bool), strict], axis=1)
    mask = np.where(keep, 0.0, -FAR)
    suffix = np.where(p >= j, -1.0, 0.0)
    return np.concatenate([far, count, mask, np.eye(P), suffix, -np.ones((P, P))], axis=1).astype(np.float32)


def trunk_kernel(nc, x_in, pre_mix, post_mix, pre_ffn, post_ffn, ab_w_in, ln_g, ln_b, sgu_w, sgu_b,
                 ab_w_out, sb_w_in, sb_w_out, ffn_w1, ffn_w2, shapes, out):
    ctx = ExitStack()
    with ctx:
        def sb(name, shape, dt=F32):
            return ctx.enter_context(nc.sbuf_tensor(name, shape, dt))

        def sem(name):
            return ctx.enter_context(nc.semaphore(name))

        x_sb = sb("x_sb", [P, TB, D])
        y_sb = sb("y_sb", [P, TB, D])
        act_hi = sb("act_hi", [P, KT, T], F32R)
        act_lo = sb("act_lo", [P, KT, T], F32R)
        hid_hi = sb("hid_hi", [P, KT, T], F32R)
        hid_lo = sb("hid_lo", [P, KT, T], F32R)
        w_raw = sb("w_raw", [P, QUARTERS, 4, NC])
        w_hi = sb("w_hi", [P, RING, 2, NC], F32R)
        w_lo = sb("w_lo", [P, RING, 2, NC], F32R)
        gpost = sb("gpost", [P, D])
        cst = sb("cst", [P, 3 * TRI + 3 * P])
        gpre = sb("gpre", [P, 4 * KT])
        qT = sb("qT", [P, HG, T])
        kT = sb("kT", [P, HG, T])
        v_sb = sb("v_sb", [P, TB, NC])
        sgu_wT = sb("sgu_wT", [P, GROUPS, P])
        sgu_bb = sb("sgu_bb", [P, GROUPS, P])
        zs = sb("zs", [P, HG, TRI])
        tmp = sb("tmp", [P, HG, TRI])
        ssy = sb("ssy", [P, TB, 4])
        ssx = sb("ssx", [P, TB, 2])
        rst = sb("rst", [P, 10])
        neg_half = sb("neg_half", [P, 2])
        bn = sb("bn", [P, TB, 2, 6])
        bna = sb("bna", [P, TB, 2])
        mx = sb("mx", [P, 2, HG])
        den = sb("den", [P, 2, HG])
        rden = sb("rden", [P, 2, HG])
        ps = ctx.enter_context(nc.psum_tensor("ps", [P, 8, 512], F32))

        far_c, count_c, mask_c = (cst[:, i * TRI:(i + 1) * TRI] for i in range(3))
        ident, suffix, ones = (cst[:, 3 * TRI + i * P:3 * TRI + (i + 1) * P] for i in range(3))
        va_n = y_sb[:, 0, :].rearrange("p (b c) -> p b c", b=TB)
        uT = y_sb[:, 1, :].rearrange("p (f t) -> p f t", t=T)
        sgu_nat = v_sb[:, :, :].rearrange("p b (g j) -> p (b g) j", j=P)
        gain_rows = tmp[0:4 * KT, 0, 0:P]
        relu_t, sq_t = qT, kT
        junk = tmp[:, 0:HG, :].rearrange("p h c -> p (h c)")
        lng_b, lnb_b = gpost[:, 0:A_W], gpost[:, A_W:D]

        def bank2(b):
            return ps[:, 2 * b:2 * b + 2, :]

        def bank2_tiles(b):
            return bank2(b).rearrange("p b (f t) -> p (b f) t", t=T)

        s_x = sem("s_x")
        s_cst = sem("s_cst")
        s_rows = sem("s_rows")
        s_sguw = sem("s_sguw")
        s_sgub = sem("s_sgub")
        raw_landed = [sem(f"raw_landed{i}") for i in range(QUARTERS)]
        s_gp = sem("s_gp")
        s_out = sem("s_out")
        hi_ready = sem("hi_ready")
        lo_ready = sem("lo_ready")
        pe_ticks = sem("pe_ticks")
        post_done = sem("post_done")
        act_post = sem("act_post")
        s_tril = sem("s_tril")
        s_half = sem("s_half")
        s_mean = sem("s_mean")
        s_pow = sem("s_pow")
        s_prepT = sem("s_prepT")
        s_prep = sem("s_prep")
        s_ssx = sem("s_ssx")
        s_ssy = sem("s_ssy")
        s_ysum = sem("s_ysum")
        s_xupd = sem("s_xupd")
        s_dve = sem("s_dve")
        s_xr = sem("s_xr")
        s_tr = sem("s_tr")
        s_ehi = sem("s_ehi")
        s_elo = sem("s_elo")
        s_y0 = sem("s_y0")
        f_relu, f_sq, f_hi = sem("f_relu"), sem("f_sq"), sem("f_hi")
        s_ln = sem("s_ln")
        s_mix, s_gate, s_ghi, s_glo = sem("s_mix"), sem("s_gate"), sem("s_ghi"), sem("s_glo")
        s_sgt = sem("s_sgt")
        s_sc = sem("s_sc")
        s_zs = sem("s_zs")
        s_sm = sem("s_sm")
        s_ex = sem("s_ex")
        s_pn = sem("s_pn")
        s_pT = sem("s_pT")
        s_pc = sem("s_pc")
        s_ab = sem("s_ab")
        s_sp = sem("s_sp")
        s_S = sem("s_S")
        s_e = sem("s_e")
        s_a = sem("s_a")
        s_o = sem("s_o")
        s_ohi = sem("s_ohi")
        s_olo = sem("s_olo")

        block = ctx.enter_context(nc.Block())

        @block.sync
        def _(sp):
            def load_quarter(u, q, w, k0, col):
                if not (isinstance(u, int) and u == 0):
                    sp.wait_ge(lo_ready, 8 * u + (2 * q - 6))
                src = w[bass.ds(k0 + 4 * P * q, 4 * P), bass.ds(col, NC)].rearrange("(k p) n -> p k n", p=P)
                sp.dma_start(w_raw[:, q, :, :], src).then_inc(raw_landed[q], 16)

            def load_unit(u, w, k0, col):
                for q in range(QUARTERS):
                    load_quarter(u, q, w, k0, col)

            def load_out(u0, w):
                at = 0
                for u, s in OUT_ORDER:
                    if s % 2 == 0:
                        sp.wait_ge(lo_ready, 8 * u0 + 2 * at - 6)
                        src = w[4 * P * (s // 2):4 * P * (s // 2 + 1), u * NC:(u + 1) * NC]
                        sp.dma_start(w_raw[:, at % 4, :, :], src.rearrange("(k p) n -> p k n", p=P)
                                     ).then_inc(raw_landed[at % 4], 16)
                        at += 1

            def load_gain(gain, layer, free_after):
                sp.wait_ge(post_done, free_after)
                sp.dma_start(gpost[:, :], gain[layer:layer + 1, :].partition_broadcast(P)
                             ).then_inc(s_gp, 16)

            def load_ffn(u0, layer):
                w1, w2 = ffn_w1[layer], ffn_w2[layer]
                with sp.Fori(0, FGROUPS - 1) as g:
                    with sp.Fori(0, 4) as j:
                        load_unit(u0 + 8 * g + j, w1, 0, (4 * g + j) * NC)
                    with sp.Fori(0, 4) as j:
                        load_unit(u0 + 8 * g + 4 + j, w2, g * D, j * NC)
                load_gain(post_ffn, layer, u0 + 1)
                g = FGROUPS - 1
                with sp.Fori(0, 4) as j:
                    load_unit(u0 + 8 * g + j, w1, 0, (4 * g + j) * NC)
                with sp.Fori(0, 4) as j:
                    load_unit(u0 + 8 * g + 4 + j, w2, g * D, j * NC)

            sp.dma_start(x_sb[:, :, :], x_in[0].rearrange("(b p) d -> p b d", p=P)).then_inc(s_x, 16)
            for u, c in enumerate((2, 3, 0, 1)):
                load_unit(u, ab_w_in[0], 0, c * NC)
            with sp.Fori(0, 2) as g:
                for i in range(3):
                    load_unit(4 + 3 * g + i, ab_w_in[0], 0, (4 + 2 * i + g) * NC)
            load_gain(post_mix, 0, 5)
            load_out(U_OUT0, ab_w_out[0])
            load_ffn(U_FFN0, 0)
            with sp.Fori(0, L1_GROUPS) as g:
                for i in range(3):
                    load_unit(U_IN1 + 3 * g + i, sb_w_in[0], 0, (4 * i + g) * NC)
            load_gain(post_mix, 1, U_IN1)
            load_out(U_OUT1, sb_w_out[0])
            load_ffn(U_FFN1, 1)
            for i in range(4):
                b, h = i // 2, i % 2
                sp.wait_ge(s_xupd, 4 * 3 + i + 1)
                sp.dma_start(out[0, b * P:(b + 1) * P, h * 1024:(h + 1) * 1024],
                             x_sb[:, b, h * 1024:(h + 1) * 1024]).then_inc(s_out, 16)
            sp.wait_ge(s_out, 64)

        @block.gpsimd
        def _(pool):
            pool.wait_ge(s_sguw, 16)
            nc.gpsimd.affine_select(out=sgu_nat, in_=sgu_nat, compare_op=ALU.is_ge, fill=0.0, base=0,
                                    pattern=[[0, GROUPS], [-1, P]], channel_multiplier=1).then_inc(s_tril, 1)
            nc.gpsimd.memset(neg_half[:, :], -0.5).then_inc(s_half, 1)
            pool.wait_ge(s_half, 1)
            done = 0

            def power(cols):
                nonlocal done
                done += 1
                pool.wait_ge(s_mean, done)
                nc.gpsimd.tensor_tensor(rst[:, cols], rst[:, cols], neg_half[:, 0:cols.stop - cols.start], ALU.pow
                                        ).then_inc(s_pow, 1)

            rs_y, rs_x0, rs_x1, rs_ln = slice(2, 4), slice(6, 7), slice(7, 8), slice(8, 10)
            for cols in (rs_x0, rs_x1, rs_ln):
                power(cols)
            for layer in range(LAYERS):
                for cols in (rs_y, rs_x0, rs_x1):
                    power(cols)
                pool.wait_ge(s_tr, 8 * (2 * layer + 2))
                nc.gpsimd.memset(y_sb[:, :, :], 0.0).then_inc(s_y0, 1)
                for cols in (rs_y, rs_x0, rs_x1) if layer == 0 else (rs_y,):
                    power(cols)

        @block.scalar
        def _(act):
            def conv(u, t):
                act.wait_ge(raw_landed[t // 2], 16 * (u + 1))
                if not (isinstance(u, int) and 8 * u + t < RING):
                    act.wait_ge(pe_ticks, 8 * u + (t - RING + 1))
                h = 2 * (t % 2)
                nc.scalar.activation(w_hi[:, t % RING, :, :], w_raw[:, t // 2, h:h + 2, :], ACT.Copy
                                     ).then_inc(hi_ready, 1)

            def conv_at(u, t):
                if t < 4:
                    conv(u, t + 4)
                elif not (isinstance(u, int) and u == UNITS - 1):
                    conv(u + 1, t - 4)

            def unit(u, post, extras=None):
                for t in range(1, TICKS):
                    for f in (extras or {}).get(t, []):
                        f()
                    conv_at(u, t)
                post()
                if not (isinstance(u, int) and u == UNITS - 1):
                    conv(u + 1, 4)

            def unit_finished(u):
                act.wait_ge(pe_ticks, 8 * u + 8)

            def nothing():
                pass

            def evacuate(k):
                for j in range(8):
                    act.wait_ge(s_tr, 8 * k + j + 1)
                    b = 2 + j if j < 6 else j - 4
                    for i in range(2):
                        kt = 2 * j + i
                        last = nc.scalar.activation(act_hi[:, kt, :], ps[:, b, i * T:(i + 1) * T], ACT.Copy,
                                                    scale=gpre[:, k * KT + kt:k * KT + kt + 1])
                    last.then_inc(s_ehi, 1)

            squares = [0, 0]

            def junk_free():
                for semaphore, n in zip((s_ssx, s_ssy), squares):
                    if n:
                        act.wait_ge(semaphore, n)

            def squares_x(k):
                for i in range(4):
                    b, h = i // 2, i % 2
                    if k:
                        act.wait_ge(s_xupd, 4 * (k - 1) + i + 1)
                    junk_free()
                    squares[0] += 1
                    nc.scalar.activation(junk[:, 0:1024], x_sb[:, b, h * 1024:(h + 1) * 1024], ACT.Square,
                                         accum_out=ssx[:, b, h:h + 1]).then_inc(s_ssx, 1)

            def transition(k):
                squares_x(k)
                evacuate(k)

            def l0_exp(grp):
                act.wait_ge(s_sm, 4 * grp + 4)
                nc.scalar.activation(zs[:, :, :], zs[:, :, :], ACT.Exp).then_inc(s_ex, 1)

            def l0_copy_pT(n):
                act.wait_ge(s_pT, n + 1)
                b = 2 * (n % 2)
                nc.scalar.activation(tmp[:, b:b + 2, :], ps[:, 6:8, 0:TRI], ACT.Copy).then_inc(s_pc, 1)

            def o_hi(n, tile):
                act.wait_ge(s_o, n + 1)
                nc.scalar.activation(hid_hi[:, bass.ds(tile, 2), :],
                                     ps[:, 6, :].rearrange("p (h t) -> p h t", t=T), ACT.Copy).then_inc(s_ohi, 1)

            def l0_extras(grp):
                return {7: [lambda: l0_exp(grp)], 12: [lambda: l0_copy_pT(2 * grp)],
                        14: [lambda: l0_copy_pT(2 * grp + 1)],
                        15: [lambda: o_hi(2 * grp, 8 + 4 * grp)],
                        18: [lambda: o_hi(2 * grp + 1, 8 + 4 * grp + 2)]}

            def l1_logs(b, grp):
                pair = 2 * grp + b
                z, t = zs[:, 2 * b:2 * b + 2, :], tmp[:, 0:2, :]
                act.wait_ge(s_zs, 4 * grp + (8 + 2 * b + 2))
                if b == 1:
                    act.wait_ge(s_sp, pair)
                nc.scalar.activation(t, z, ACT.Abs).then_inc(s_ab, 1)
                act.wait_ge(s_ab, 3 * pair + 1)
                nc.scalar.activation(t, t, ACT.Exp, scale=-1.0).then_inc(s_ab, 1)
                act.wait_ge(s_ab, 3 * pair + 2)
                nc.scalar.activation(t, t, ACT.Ln, bias=1.0).then_inc(s_ab, 1)

            def l1_weights(b, grp):
                z = zs[:, 2 * b:2 * b + 2, :]
                act.wait_ge(s_e, 2 * grp + (b + 1))
                nc.scalar.activation(z, z, ACT.Exp).then_inc(s_a, 1)

            def l1_extras(grp):
                return {5: [lambda: l1_logs(0, grp)], 10: [lambda: l1_weights(0, grp)],
                        11: [lambda: l1_logs(1, grp)],
                        12: [lambda: o_hi(2 * grp + 4, 4 * grp)],
                        15: [lambda: l1_weights(1, grp)], 18: [lambda: o_hi(2 * grp + 5, 4 * grp + 2)]}

            def qkv_group(u, extras):
                for i in range(3):
                    unit(u + i, nothing, {t - 8 * i: f for t, f in extras.items() if 8 * i < t < 8 * i + 8})

            def sum_squares_y(src, c, n):
                for b in range(TB):
                    junk_free()
                    squares[1] += 1
                    nc.scalar.activation(junk[:, 0:NC], src[b], ACT.Square, accum_out=ssy[:, b, c:c + 1]
                                         ).then_inc(s_ssy, 1)

            def out_phase(u0, extras, first_post):
                for t in range(1, 32):
                    for f in extras.get(t, []):
                        f()
                    if t in OUT_POST:
                        c = OUT_POST[t]
                        act.wait_ge(pe_ticks, 8 * u0 + t)
                        sum_squares_y([ps[:, 2 * OUT_BUF[c] + b, :] for b in range(TB)], c, 0)
                    conv_at(u0 + t // 8, t % 8)
                unit_finished(u0 + 3)
                sum_squares_y([ps[:, b, :] for b in range(TB)], 3, 0)

            def ffn(u0, layer):
                f0 = 16 * layer

                def up(g, jj, par):
                    u, f = u0 + 8 * g + 2 * jj + par, f0 + 4 * g + 2 * jj + par

                    def post():
                        unit_finished(u)
                        nc.scalar.activation(relu_t[:, :, :], bank2_tiles(par), ACT.Relu).then_inc(f_relu, 1)
                        act.wait_ge(f_sq, f + 1)
                        nc.scalar.activation(hid_hi[:, bass.ds(8 * jj + 4 * par, 4), :], sq_t[:, :, :], ACT.Copy
                                             ).then_inc(f_hi, 1)
                    unit(u, post)

                def group_up(g):
                    with act.Fori(0, 2) as jj:
                        for par in range(2):
                            up(g, jj, par)

                with act.Fori(0, FGROUPS - 1) as g:
                    group_up(g)
                    with act.Fori(0, 2) as jj:
                        for par in range(2):
                            unit(u0 + 8 * g + 4 + 2 * jj + par, nothing)
                group_up(FGROUPS - 1)
                for j in range(4):
                    u = u0 + 8 * (FGROUPS - 1) + 4 + j

                    def post(j=j):
                        act.wait_ge(s_ysum, 4 * layer + j + 1)
                        sum_squares_y([y_sb[:, b, j * NC:(j + 1) * NC] for b in range(TB)], j, 0)
                        if j == 3:
                            after_ffn(layer)
                    unit(u, post)

            def after_ffn(layer):
                if layer == 0:
                    transition(2)

            act.dma_start(cst[:, :], shapes).then_inc(s_cst, 16)
            for i, (g, l) in enumerate(((pre_mix, 0), (pre_ffn, 0), (pre_mix, 1), (pre_ffn, 1))):
                act.dma_start(tmp[i * KT:(i + 1) * KT, 0, 0:P], g[l].rearrange("(k p) -> k p", p=P)
                              ).then_inc(s_rows, 16)
            act.dma_start(sgu_nat, sgu_w[0].rearrange("g i j -> i g j")).then_inc(s_sguw, 16)
            act.dma_start(sgu_bb[:, :, :].rearrange("p g i -> p (g i)"),
                          sgu_b[0:1].rearrange("o g i -> o (g i)").partition_broadcast(P)).then_inc(s_sgub, 16)
            act.dma_start(lng_b, ln_g[0:1, :].partition_broadcast(P)).then_inc(s_sgub, 16)
            act.dma_start(lnb_b, ln_b[0:1, :].partition_broadcast(P)).then_inc(s_sgub, 16)
            act.wait_ge(s_prepT, 1)
            nc.scalar.activation(gpre[:, :], ps[:, 5, 0:4 * KT], ACT.Copy).then_inc(s_prep, 1)
            act.wait_ge(s_prepT, 3)
            nc.scalar.activation(sgu_wT[:, :, :], ps[:, 6:8, :].rearrange("p b (g i) -> p (b g) i", i=P), ACT.Copy
                                 ).then_inc(s_prep, 1)
            act.wait_ge(s_x, 16)
            act.wait_ge(s_prep, 2)
            squares_x(0)
            for t in range(4):
                conv(0, t)
            evacuate(0)
            conv(0, 4)

            def gelu_v(j):
                unit_finished(j)
                nc.scalar.activation(va_n[:, :, j * NC:(j + 1) * NC], bank2(j), ACT.Gelu).then_inc(act_post, 1)

            def gelu_u(j):
                unit_finished(2 + j)
                nc.scalar.activation(uT[:, 4 * j:4 * j + 4, :], bank2_tiles(j), ACT.Gelu).then_inc(act_post, 1)

            def gate_hi(m):
                act.wait_ge(s_gate, m + 1)
                nc.scalar.activation(hid_hi[:, 2 * m:2 * m + 2, :],
                                     gated, ACT.Copy
                                     ).then_inc(s_ghi, 1)

            gated = junk[:, 512:1024].rearrange("p (g t) -> p g t", t=T)
            for j in range(2):
                unit(j, lambda j=j: gelu_v(j))
            for j in range(2):
                unit(2 + j, lambda j=j: gelu_u(j))
            qkv_group(4, {m + 1: [lambda m=m: gate_hi(m)] for m in range(4)})
            qkv_group(7, l0_extras(0))
            out_phase(U_OUT0, l0_extras(1), None)
            transition(1)
            conv(U_FFN0, 4)
            ffn(U_FFN0, 0)

            qkv_group(U_IN1, {})
            with act.Fori(1, L1_GROUPS) as g:
                qkv_group(U_IN1 + 3 * g, l1_extras(g - 1))
            out_phase(U_OUT1, l1_extras(L1_GROUPS - 1), None)
            transition(3)
            conv(U_FFN1, 4)
            ffn(U_FFN1, 1)

        @block.vector
        def _(dve):
            steps, powers = [0], [0]

            def chain(ins):
                steps[0] += 1
                ins.then_inc(s_dve, 1)
                dve.wait_ge(s_dve, steps[0])

            def conv(u, t):
                dve.wait_ge(hi_ready, 8 * u + (t + 1))
                h = 2 * (t % 2)
                nc.vector.tensor_tensor(w_lo[:, t % RING, :, :], w_raw[:, t // 2, h:h + 2, :],
                                        w_hi[:, t % RING, :, :].bitcast(F32), ALU.subtract).then_inc(lo_ready, 1)

            def conv_at(u, t):
                if t < 4:
                    conv(u, t + 4)
                elif not (isinstance(u, int) and u == UNITS - 1):
                    conv(u + 1, t - 4)

            def unit(u, post, extras=None):
                for t in range(1, TICKS):
                    for f in (extras or {}).get(t, []):
                        f()
                    conv_at(u, t)
                post()
                if not (isinstance(u, int) and u == UNITS - 1):
                    conv(u + 1, 4)

            def unit_finished(u):
                dve.wait_ge(pe_ticks, 8 * u + 8)

            def rsqrt(dst, src, scale, eps):
                nc.vector.tensor_scalar(dst, src, scale, eps, ALU.mult, ALU.add).then_inc(s_mean, 1)
                powers[0] += 1
                dve.wait_ge(s_pow, powers[0])

            def update_x(k):
                dve.wait_ge(s_ssy, 8 * k)
                chain(nc.vector.tensor_reduce(rst[:, 0:2], ssy[:, :, :], AX.X, ALU.add))
                rsqrt(rst[:, 2:4], rst[:, 0:2], 1.0 / D, RMS_EPS)
                for i in range(4):
                    b, h = i // 2, i % 2
                    xs = x_sb[:, b, h * 1024:(h + 1) * 1024]
                    nc.vector.scalar_tensor_tensor(xs, y_sb[:, b, h * 1024:(h + 1) * 1024], rst[:, 2 + b:3 + b], xs,
                                                   ALU.mult, ALU.add).then_inc(s_xupd, 1)

            def normed_rows(k):
                for b in range(TB):
                    dve.wait_ge(s_ssx, 4 * k + 2 * b + 2)
                    chain(nc.vector.tensor_reduce(rst[:, 4 + b:5 + b], ssx[:, b, :], AX.X, ALU.add))
                    rsqrt(rst[:, 6 + b:7 + b], rst[:, 4 + b:5 + b], 1.0 / D, RMS_EPS)
                    if k:
                        dve.wait_ge(s_xupd, 4 * (k - 1) + 2 * b + 2)
                    nc.vector.tensor_scalar(y_sb[:, b, :], x_sb[:, b, :], rst[:, 6 + b:7 + b], None, ALU.mult
                                            ).then_inc(s_xr, 1)

            def evacuate(k):
                for j in range(8):
                    dve.wait_ge(s_ehi, 8 * k + j + 1)
                    b = 2 + j if j < 6 else j - 4
                    for i in range(2):
                        kt = 2 * j + i
                        last = nc.vector.scalar_tensor_tensor(
                            act_lo[:, kt, :], ps[:, b, i * T:(i + 1) * T], gpre[:, k * KT + kt:k * KT + kt + 1],
                            act_hi[:, kt, :].bitcast(F32), ALU.mult, ALU.subtract)
                    last.then_inc(s_elo, 1)

            def transition(k):
                update_x(k)
                normed_rows(k)
                evacuate(k)

            def l0_scores(h, head):
                dve.wait_ge(s_sc, head + 1)
                nc.vector.scalar_tensor_tensor(zs[:, h, :], far_c, -(2.0 ** -(head + 1)), ps[:, 6 + h % 2, 0:TRI],
                                               ALU.mult, ALU.add).then_inc(s_zs, 1)

            def halves(t):
                return t[:, :, 0:P], t[:, :, P:TRI]

            def l0_max(grp):
                dve.wait_ge(s_zs, 4 * grp + 4)
                for i, z in enumerate(halves(zs)):
                    nc.vector.tensor_reduce(mx[:, i, :], z, AX.X, ALU.max).then_inc(s_sm, 1)

            def l0_less_max(grp):
                dve.wait_ge(s_sm, 4 * grp + 2)
                for i, z in enumerate(halves(zs)):
                    m = mx[:, i, :].unsqueeze(2).broadcast_to([P, HG, z.shape[2]])
                    nc.vector.tensor_tensor(z, z, m, ALU.subtract).then_inc(s_sm, 1)

            def l0_count(grp):
                dve.wait_ge(s_ex, grp + 1)
                chain(nc.vector.tensor_tensor(zs[:, :, :], zs[:, :, :],
                                              count_c.unsqueeze(1).broadcast_to([P, HG, TRI]), ALU.mult))

            def l0_normalise(grp):
                for i, z in enumerate(halves(zs)):
                    chain(nc.vector.tensor_reduce(den[:, i, :], z, AX.X, ALU.add))
                chain(nc.vector.reciprocal(rden[:, :, :], den[:, :, :]))
                for i, z in enumerate(halves(zs)):
                    m = rden[:, i, :].unsqueeze(2).broadcast_to([P, HG, z.shape[2]])
                    nc.vector.tensor_tensor(z, z, m, ALU.mult).then_inc(s_pn, 1)

            def o_lo(n, tile):
                dve.wait_ge(s_ohi, n + 1)
                nc.vector.tensor_tensor(hid_lo[:, bass.ds(tile, 2), :], ps[:, 6, :].rearrange("p (h t) -> p h t", t=T),
                                        hid_hi[:, bass.ds(tile, 2), :].bitcast(F32), ALU.subtract).then_inc(s_olo, 1)

            def l0_extras(grp):
                e = {1 + h: [lambda h=h: l0_scores(h, 4 * grp + h)] for h in range(4)}
                e.update({5: [lambda: l0_max(grp)], 6: [lambda: l0_less_max(grp)], 9: [lambda: l0_count(grp)],
                          10: [lambda: l0_normalise(grp)], 15: [lambda: o_lo(2 * grp, 8 + 4 * grp)],
                          18: [lambda: o_lo(2 * grp + 1, 8 + 4 * grp + 2)]})
                return e

            def l1_scores(h, grp):
                dve.wait_ge(s_sc, 4 * grp + (8 + h + 1))
                nc.vector.tensor_tensor(zs[:, h, :], ps[:, 6 + h % 2, 0:TRI], mask_c, ALU.add).then_inc(s_zs, 1)

            def l1_softplus(b, grp):
                dve.wait_ge(s_ab, 6 * grp + 3 * b + 3)
                nc.vector.scalar_tensor_tensor(tmp[:, 2:4, :], zs[:, 2 * b:2 * b + 2, :], 0.0, tmp[:, 0:2, :],
                                               ALU.max, ALU.add).then_inc(s_sp, 1)

            def l1_exponent(b, grp):
                dve.wait_ge(s_S, 2 * grp + (b + 1))
                z = zs[:, 2 * b:2 * b + 2, :]
                nc.vector.tensor_tensor(z, z, ps[:, 6:8, 0:TRI], ALU.add).then_inc(s_e, 1)

            def l1_extras(grp):
                e = {1 + h: [lambda h=h: l1_scores(h, grp)] for h in range(4)}
                e.update({6: [lambda: l1_softplus(0, grp)], 9: [lambda: l1_exponent(0, grp)],
                          12: [lambda: o_lo(2 * grp + 4, 4 * grp), lambda: l1_softplus(1, grp)],
                          14: [lambda: l1_exponent(1, grp)],
                          18: [lambda: o_lo(2 * grp + 5, 4 * grp + 2)]})
                return e

            def qkv_group(u, extras):
                def post_q():
                    unit_finished(u)
                    nc.vector.tensor_scalar(qT[:, :, :], bank2_tiles(0), SCALE, None, ALU.mult).then_inc(post_done, 1)

                def post_k():
                    unit_finished(u + 1)
                    nc.vector.tensor_copy(kT[:, :, :], bank2_tiles(1)).then_inc(post_done, 1)

                def post_v():
                    unit_finished(u + 2)
                    nc.vector.tensor_copy(v_sb[:, :, :], bank2(2)).then_inc(post_done, 1)

                for i, post in enumerate((post_q, post_k, post_v)):
                    unit(u + i, post, {t - 8 * i: f for t, f in extras.items() if 8 * i < t < 8 * i + 8})

            def out_phase(u0, extras, k):
                def post(c):
                    dve.wait_ge(s_ssy, 8 * (k - 1) + 2 * c + 2)
                    dve.wait_ge(s_gp, 16 * k)
                    g = gpost[:, c * NC:(c + 1) * NC].unsqueeze(1).broadcast_to([P, TB, NC])
                    nc.vector.tensor_tensor(y_sb[:, :, c * NC:(c + 1) * NC], bank2(OUT_BUF[c]), g, ALU.mult
                                            ).then_inc(post_done, 1)

                for t in range(1, 32):
                    for f in extras.get(t, []):
                        f()
                    if t in OUT_POST:
                        post(OUT_POST[t])
                    conv_at(u0 + t // 8, t % 8)
                post(3)

            def ffn(u0, layer):
                f0 = 16 * layer

                def up(g, jj, par):
                    u, f = u0 + 8 * g + 2 * jj + par, f0 + 4 * g + 2 * jj + par

                    def post():
                        dve.wait_ge(f_relu, f + 1)
                        nc.vector.scalar_tensor_tensor(sq_t[:, :, :], bank2_tiles(par), 0.0, relu_t[:, :, :],
                                                       ALU.max, ALU.mult).then_inc(f_sq, 1)
                        dve.wait_ge(f_hi, f + 1)
                        tiles = bass.ds(8 * jj + 4 * par, 4)
                        nc.vector.tensor_tensor(hid_lo[:, tiles, :], sq_t[:, :, :], hid_hi[:, tiles, :].bitcast(F32),
                                                ALU.subtract).then_inc(post_done, 1)
                    unit(u, post)

                def group_up(g):
                    with dve.Fori(0, 2) as jj:
                        for par in range(2):
                            up(g, jj, par)

                def add_y(u, chunk, par):
                    unit_finished(u)
                    dve.wait_ge(post_done, u)
                    ys = y_sb[:, :, bass.ds(chunk, NC)]
                    return nc.vector.tensor_tensor(ys, ys, bank2(par), ALU.add)

                with dve.Fori(0, FGROUPS - 1) as g:
                    group_up(g)
                    dve.wait_ge(s_y0, layer + 1)
                    with dve.Fori(0, 2) as jj:
                        for par in range(2):
                            u = u0 + 8 * g + 4 + 2 * jj + par
                            unit(u, lambda: add_y(u, 2 * NC * jj + NC * par, par).then_inc(post_done, 1))
                group_up(FGROUPS - 1)
                for j in range(4):
                    u = u0 + 8 * (FGROUPS - 1) + 4 + j

                    def post(j=j, u=u):
                        add_y(u, j * NC, j % 2).then_inc(s_ysum, 1)
                        k = 2 * layer + 2
                        dve.wait_ge(s_ssy, 8 * (k - 1) + 2 * j + 2)
                        dve.wait_ge(s_gp, 16 * k)
                        ys = y_sb[:, :, j * NC:(j + 1) * NC]
                        g = gpost[:, j * NC:(j + 1) * NC].unsqueeze(1).broadcast_to([P, TB, NC])
                        nc.vector.tensor_tensor(ys, ys, g, ALU.mult).then_inc(post_done, 1)
                        if j == 3:
                            dve.wait_ge(post_done, u + 1)
                            if layer == 0:
                                transition(2)
                            else:
                                update_x(4)
                    unit(u, post)

            for t in range(4):
                if t == 0:
                    normed_rows(0)
                conv(0, t)
            evacuate(0)
            conv(0, 4)

            def stats_v(j):
                dve.wait_ge(act_post, j + 1)
                for b in range(TB):
                    last = nc.vector.bn_stats(bn[:, b, j, :], va_n[:, b, j * NC:(j + 1) * NC])
                last.then_inc(post_done, 1)

            def layernorm_v(step):
                if step == 0:
                    dve.wait_ge(post_done, 2)
                    for b in range(TB):
                        chain(nc.vector.bn_aggr(bna[:, b, :], bn[:, b, :, :]))
                    rsqrt(rst[:, 8:10], bna[:, :, 1], 1.0, LN_EPS)
                    for b in range(TB):
                        nc.vector.tensor_scalar(va_n[:, b, :], va_n[:, b, :], bna[:, b, 0:1], rst[:, 8 + b:9 + b],
                                                ALU.subtract, ALU.mult).then_inc(s_ln, 1)
                else:
                    dve.wait_ge(s_ln, step + 1)
                    dve.wait_ge(s_sgub, 48)
                    g = (lng_b if step == 1 else lnb_b).unsqueeze(1).broadcast_to([P, TB, A_W])
                    nc.vector.tensor_tensor(va_n, va_n, g, ALU.mult if step == 1 else ALU.add).then_inc(s_ln, 1)

            def post_u(j):
                dve.wait_ge(act_post, 3 + j)
                dve.sem_inc(post_done, 1)

            mixed = junk[:, 0:512].rearrange("p (g c i) -> p g c i", g=2, i=P)
            gated = junk[:, 512:1024].rearrange("p (g t) -> p g t", t=T)

            def gate(m):
                dve.wait_ge(s_mix, m + 1)
                dve.wait_ge(act_post, 4)
                bias = sgu_bb[:, 2 * m:2 * m + 2, :].unsqueeze(2).broadcast_to([P, 2, TB, P])
                nc.vector.tensor_tensor(mixed, ps[:, 6 + m % 2, :].rearrange("p (g c i) -> p g c i", g=2, i=P), bias,
                                        ALU.add).then_inc(s_sgt, 1)
                dve.wait_ge(s_sgt, m + 1)
                nc.vector.tensor_tensor(gated, junk[:, 0:512].rearrange("p (g t) -> p g t", t=T),
                                        uT[:, 2 * m:2 * m + 2, :], ALU.mult).then_inc(s_gate, 1)

            def gate_lo(m):
                dve.wait_ge(s_ghi, m + 1)
                nc.vector.tensor_tensor(hid_lo[:, 2 * m:2 * m + 2, :], gated,
                                        hid_hi[:, 2 * m:2 * m + 2, :].bitcast(F32), ALU.subtract).then_inc(s_glo, 1)

            for j in range(2):
                unit(j, lambda j=j: stats_v(j))
            unit(2, lambda: post_u(0), {1 + i: [lambda i=i: layernorm_v(i)] for i in range(3)})
            unit(3, lambda: post_u(1))
            gates = {1: [lambda: gate(0)], 5: [lambda: gate_lo(3)]}
            for m in range(1, 4):
                gates[1 + m] = [lambda m=m: gate_lo(m - 1), lambda m=m: gate(m)]
            qkv_group(4, gates)
            qkv_group(7, l0_extras(0))
            out_phase(U_OUT0, l0_extras(1), 1)
            transition(1)
            conv(U_FFN0, 4)
            ffn(U_FFN0, 0)

            qkv_group(U_IN1, {})
            with dve.Fori(1, L1_GROUPS) as g:
                qkv_group(U_IN1 + 3 * g, l1_extras(g - 1))
            out_phase(U_OUT1, l1_extras(L1_GROUPS - 1), 3)
            transition(3)
            conv(U_FFN1, 4)
            ffn(U_FFN1, 1)

        @block.tensor
        def _(pe):
            def mm(dst, lhsT, rhs, start, stop):
                return nc.tensor.matmul(dst, lhsT, rhs, start=start, stop=stop, skip_group_check=True)

            def tick_tokens(buf, s, slot, hi, lo, ready):
                pe.wait_ge(lo_ready, ready)
                for i in range(2):
                    kt = 2 * s + i
                    for b in range(TB):
                        dst, tok = ps[:, 2 * buf + b, :], slice(b * P, (b + 1) * P)
                        mm(dst, hi[:, kt, tok], w_hi[:, slot, i, :], kt == 0, False)
                        mm(dst, hi[:, kt, tok], w_lo[:, slot, i, :], False, False)
                        last = mm(dst, lo[:, kt, tok], w_hi[:, slot, i, :], False, kt == KT - 1)
                last.then_inc(pe_ticks, 1)

            def tick_features(buf, s, slot, hi, lo, ready):
                pe.wait_ge(lo_ready, ready)
                for i in range(2):
                    kt = 2 * s + i
                    for f in range(4):
                        dst, cols = ps[:, 2 * buf + f // 2, (f % 2) * T:(f % 2 + 1) * T], slice(f * P, (f + 1) * P)
                        mm(dst, w_hi[:, slot, i, cols], hi[:, kt, :], kt == 0 and f % 2 == 0, False)
                        mm(dst, w_hi[:, slot, i, cols], lo[:, kt, :], False, False)
                        last = mm(dst, w_lo[:, slot, i, cols], hi[:, kt, :], False, kt == KT - 1)
                last.then_inc(pe_ticks, 1)

            def unit(u, tick, buf, hi=act_hi, lo=act_lo, fresh=None, extras=None, before=None, posts=None):
                need = u if fresh is not None or posts == "all" else u - 1
                if not (isinstance(need, int) and need <= 0):
                    pe.wait_ge(post_done, need)
                for s in range(TICKS):
                    for f in (extras or {}).get(s, []):
                        f()
                    if fresh is not None:
                        pe.wait_ge(s_elo, 8 * fresh + s + 1)
                    if before is not None:
                        before(s)
                    tick(buf, s, s % RING, hi, lo, 8 * u + (s + 1))

            def transposes(k, u):
                if u:
                    pe.wait_ge(post_done, u)
                else:
                    pe.wait_ge(s_prep, 2)

                def half(j, b):
                    bank = 2 + j if j < 6 else j - 4
                    for i in range(2):
                        kt = 2 * j + i
                        last = nc.tensor.transpose(ps[:, bank, i * T + b * P:i * T + (b + 1) * P],
                                                   y_sb[:, b, kt * P:(kt + 1) * P], ident)
                    return last

                for b in range(TB):
                    pe.wait_ge(s_xr, 2 * k + b + 1)
                    for j in range(6):
                        last = half(j, b)
                        if b == 1:
                            last.then_inc(s_tr, 1)
                for j in (6, 7):
                    pe.wait_ge(s_elo, 8 * k + j - 5)
                    half(j, 0)
                    half(j, 1).then_inc(s_tr, 1)

            def l0_scores(h, head):
                if h >= 2:
                    pe.wait_ge(s_zs, head - 1)
                if h == 0:
                    pe.wait_ge(post_done, 7 + 3 * (head // 4))
                b = 6 + h % 2
                mm(ps[:, b, 0:P], qT[:, h, 0:P], kT[:, h, 0:P], True, True)
                mm(ps[:, b, P:TRI], qT[:, h, P:T], kT[:, h, :], True, True).then_inc(s_sc, 1)

            def l0_pT(n):
                if n % 2 == 0:
                    pe.wait_ge(s_pn, n + 2)
                else:
                    pe.wait_ge(s_pc, n)
                for i in range(2):
                    for c in range(3):
                        last = nc.tensor.transpose(ps[:, 6 + i, c * P:(c + 1) * P],
                                                   zs[:, 2 * (n % 2) + i, c * P:(c + 1) * P], ident)
                last.then_inc(s_pT, 1)

            def values(n, b, w):
                for i in range(2):
                    vh = slice((2 * b + i) * P, (2 * b + i + 1) * P)
                    mm(ps[:, 6, i * T:(i + 1) * T], v_sb[:, 0, vh], w[:, i, 0:T], i == 0, False)
                    last = mm(ps[:, 6, i * T + P:(i + 1) * T], v_sb[:, 1, vh], w[:, i, T:TRI], False, True)
                last.then_inc(s_o, 1)

            def l0_values(n, b):
                pe.wait_ge(s_pc, n - n % 2 + 2)
                if b == 1:
                    pe.wait_ge(s_olo, n)
                values(n, b, tmp[:, 2 * b:2 * b + 2, :])

            def l0_extras(grp):
                e = {1 + h: [lambda h=h: l0_scores(h, 4 * grp + h)] for h in range(4)}
                e.update({11: [lambda: l0_pT(2 * grp)], 13: [lambda: l0_pT(2 * grp + 1)],
                          15: [lambda: l0_values(2 * grp, 0)], 17: [lambda: l0_values(2 * grp + 1, 1)]})
                return e

            def l1_scores(h, grp):
                if h >= 2:
                    pe.wait_ge(s_zs, 4 * grp + (8 + h - 1))
                if h == 0:
                    pe.wait_ge(post_done, 3 * grp + (U_IN1 + 3))
                    pe.wait_ge(s_olo, 2 * grp + 4)
                b = 6 + h % 2
                mm(ps[:, b, 0:T], kT[:, h, 0:P], qT[:, h, :], True, True)
                mm(ps[:, b, T:TRI], kT[:, h, P:T], qT[:, h, P:T], True, True).then_inc(s_sc, 1)

            def l1_suffix(b, grp):
                pe.wait_ge(s_sp, 2 * grp + (b + 1))
                pe.wait_ge(s_zs, 4 * grp + (8 + 4))
                if b == 1:
                    pe.wait_ge(s_olo, 2 * grp + 5)
                for i in range(2):
                    z, dst = tmp[:, 2 + i, :], ps[:, 6 + i, :]
                    mm(dst[:, 0:T], suffix, z[:, 0:T], True, False)
                    mm(dst[:, P:T], ones, z[:, T:TRI], False, True)
                    last = mm(dst[:, T:TRI], suffix, z[:, T:TRI], False, True)
                last.then_inc(s_S, 1)

            def l1_values(b, grp):
                pe.wait_ge(s_a, 2 * grp + (b + 1))
                values(None, b, zs[:, 2 * b:2 * b + 2, :])

            def l1_extras(grp):
                e = {1 + h: [lambda h=h: l1_scores(h, grp)] for h in range(4)}
                e.update({7: [lambda: l1_suffix(0, grp)], 11: [lambda: l1_values(0, grp)],
                          13: [lambda: l1_suffix(1, grp)], 17: [lambda: l1_values(1, grp)]})
                return e

            def qkv_group(u, extras, fresh=None):
                for i, tick in enumerate((tick_features, tick_features, tick_tokens)):
                    unit(u + i, tick, i, fresh=fresh if i == 0 else None,
                         extras={t - 8 * i: f for t, f in extras.items() if 8 * i <= t < 8 * i + 8})

            def out_phase(u0, extras, ready):
                for t, (u, s) in enumerate(OUT_ORDER):
                    for f in extras.get(t, []):
                        f()
                    if s == 0:
                        pe.wait_ge(post_done, u0 + (1 if u == 3 else 0 if u == 2 else -1))
                    if t < 6 or t in (18, 19):
                        for semaphore, value in ready(s):
                            pe.wait_ge(semaphore, value)
                    tick_tokens(OUT_BUF[u], s, t % RING, hid_hi, hid_lo, 8 * u0 + t + 1)

            def ffn(u0, k):
                def up(g, first):
                    with pe.Fori(0, 2) as jj:
                        for par in range(2):
                            unit(u0 + 8 * g + 2 * jj + par, tick_features, par)

                def down(g):
                    def hidden_ready(s):
                        if s % 2 == 0:
                            pe.wait_ge(post_done, u0 + 8 * g + (s // 2 + 1))

                    with pe.Fori(0, 2) as jj:
                        for par in range(2):
                            unit(u0 + 8 * g + 4 + 2 * jj + par, tick_tokens, par, hid_hi, hid_lo,
                                 before=hidden_ready)

                unit(u0, tick_features, 0, fresh=k)
                unit(u0 + 1, tick_features, 1)
                for par in range(2):
                    unit(u0 + 2 + par, tick_features, par)
                down(0)
                with pe.Fori(1, FGROUPS) as g:
                    up(g, False)
                    down(g)

            pe.wait_ge(s_cst, 16)
            pe.wait_ge(s_rows, 64)
            nc.tensor.transpose(ps[:, 5, 0:4 * KT], gain_rows, ident[0:4 * KT, 0:4 * KT]).then_inc(s_prepT, 1)
            pe.wait_ge(s_tril, 1)
            for g in range(GROUPS):
                last = nc.tensor.transpose(ps[:, 6 + g // 4, (g % 4) * P:(g % 4 + 1) * P], sgu_nat[:, g, :], ident)
                if g % 4 == 3:
                    last.then_inc(s_prepT, 1)
            transposes(0, 0)

            def mix(m):
                if m == 0:
                    pe.wait_ge(s_ln, 4)
                if m >= 2:
                    pe.wait_ge(s_sgt, m - 1)
                for i in range(2):
                    g = 2 * m + i
                    for c in range(TB):
                        last = mm(ps[:, 6 + m % 2, i * T + c * P:i * T + (c + 1) * P],
                                  va_n[:, c, g * P:(g + 1) * P], sgu_wT[:, g, :], True, True)
                last.then_inc(s_mix, 1)

            unit(0, tick_tokens, 0, fresh=0)
            unit(1, tick_tokens, 1)
            unit(2, tick_features, 0)
            unit(3, tick_features, 1)
            qkv_group(4, {1 + m: [lambda m=m: mix(m)] for m in range(4)})
            qkv_group(7, l0_extras(0))

            def ready0(s):
                if s < 4:
                    return [(s_glo, s + 1)]
                return [(s_olo, s - 3)]
            out_phase(U_OUT0, l0_extras(1), ready0)
            transposes(1, U_FFN0)
            ffn(U_FFN0, 1)

            transposes(2, U_IN1)
            qkv_group(U_IN1, {}, fresh=2)
            with pe.Fori(1, L1_GROUPS) as g:
                qkv_group(U_IN1 + 3 * g, l1_extras(g - 1))
            out_phase(U_OUT1, l1_extras(L1_GROUPS - 1), lambda s: [(s_olo, 4 + s + 1)])
            transposes(3, U_FFN1)
            ffn(U_FFN1, 3)


_INS = ['x', 'norm_pre_mix', 'norm_post_mix', 'norm_pre_ffn', 'norm_post_ffn', 'ab_w_in', 'sgu_ln_g', 'sgu_ln_b',
        'sgu_w', 'sgu_b', 'ab_w_out', 'sb_w_in', 'sb_w_out', 'ffn_w1', 'ffn_w2']
_OUT = ((1, T, D), 'float32')


def kernel(**inputs):
    import numpy as _np
    import concourse.bacc as _bacc
    from concourse import mybir as _mybir
    from concourse.bass_utils import run_bass_kernel_spmd as _run

    nc = _bacc.Bacc("TRN2", target_bir_lowering=False, num_devices=1)
    arrays, args = {}, []
    for name in _INS:
        arrays[f"in_{name}_dram"] = _np.ascontiguousarray(inputs[name])
    arrays["shape_constants_dram"] = shape_constants()
    for name, a in arrays.items():
        args.append(nc.dram_tensor(name, a.shape, _mybir.dt.from_np(a.dtype), kind="ExternalInput").ap())
    args.append(nc.dram_tensor("out_dram", _OUT[0], _mybir.dt.from_np(_np.dtype(_OUT[1])), kind="ExternalOutput").ap())
    trunk_kernel(nc, *args)
    r = _run(nc, [arrays], core_ids=[0])
    return r.results[0]["out_dram"]
```

```python
from contextlib import ExitStack

import numpy as np

import concourse.bass as bass
from concourse import mybir

F32 = mybir.dt.float32
F32R = mybir.dt.float32r
ALU = mybir.AluOpType
ACT = mybir.ActivationFunctionType
AX = mybir.AxisListType

P = 128
T = 256
TB = T // P
D = 2048
KT = D // P
NC = 512
TICKS = KT // 2
QUARTERS = 4
RING = 4
A_W = D // 2
GROUPS = A_W // P
LAYERS = 2
DFF = 4 * D
FGROUPS = DFF // D
HG = 4
L0_HEADS = 8
L1_GROUPS = 4
SCALE = float(P) ** -0.5
RMS_EPS = 1e-6
LN_EPS = 1e-5
TRI = 3 * P
FAR = 1e30
ROW_HALVES = [(b, slice(h * D // 2, (h + 1) * D // 2)) for b in range(TB) for h in range(2)]

U_IN0, U_OUT0, U_FFN0, U_IN1, U_OUT1, U_FFN1, UNITS = 0, 10, 14, 46, 58, 62, 94
OUT_ORDER = ([(u, s) for u in range(3) for s in range(6)] + [(u, s) for u in range(3) for s in (6, 7)]
             + [(3, s) for s in range(8)])
OUT_BUF = [0, 1, 2, 0]
OUT_POST = {20: 0, 22: 1, 24: 2}


def shape_constants():
    p = np.arange(P)[:, None]
    j = np.arange(P)[None, :]
    dist = np.concatenate([p - j, p + P - j, p - j], axis=1)
    causal = dist >= 0
    count = (causal & (dist <= 128)).astype(np.float32) + (causal & (dist % 4 == 0)) + (causal & (dist % 16 == 0))
    far = np.where(count > 0, dist, FAR)
    strict = p < j
    keep = np.concatenate([strict, np.ones((P, P), bool), strict], axis=1)
    mask = np.where(keep, 0.0, -FAR)
    suffix = np.where(p >= j, -1.0, 0.0)
    return np.concatenate([far, count, mask, np.eye(P), suffix, -np.ones((P, P))], axis=1).astype(np.float32)


def trunk_kernel(nc, x_in, pre_mix, post_mix, pre_ffn, post_ffn, ab_w_in, ln_g, ln_b, sgu_w, sgu_b,
                 ab_w_out, sb_w_in, sb_w_out, ffn_w1, ffn_w2, shapes, out):
    ctx = ExitStack()
    with ctx:
        def sb(name, shape, dt=F32):
            return ctx.enter_context(nc.sbuf_tensor(name, shape, dt))

        def sem(name):
            return ctx.enter_context(nc.semaphore(name))

        x_sb = sb("x_sb", [P, TB, D])
        y_sb = sb("y_sb", [P, TB, D])
        act_hi = sb("act_hi", [P, KT, T], F32R)
        act_lo = sb("act_lo", [P, KT, T], F32R)
        hid_hi = sb("hid_hi", [P, KT, T], F32R)
        hid_lo = sb("hid_lo", [P, KT, T], F32R)
        w_raw = sb("w_raw", [P, QUARTERS, 4, NC])
        w_hi = sb("w_hi", [P, RING, 2, NC], F32R)
        w_lo = sb("w_lo", [P, RING, 2, NC], F32R)
        gpost = sb("gpost", [P, D])
        cst = sb("cst", [P, 3 * TRI + 3 * P])
        gpre = sb("gpre", [P, 4 * KT])
        qT = sb("qT", [P, HG, T])
        kT = sb("kT", [P, HG, T])
        v_sb = sb("v_sb", [P, TB, NC])
        sgu_wT = sb("sgu_wT", [P, GROUPS, P])
        sgu_bb = sb("sgu_bb", [P, GROUPS, P])
        zs = sb("zs", [P, HG, TRI])
        tmp = sb("tmp", [P, HG, TRI])
        ssy = sb("ssy", [P, TB, 4])
        ssx = sb("ssx", [P, TB, 2])
        rst = sb("rst", [P, 10])
        neg_half = sb("neg_half", [P, 2])
        bn = sb("bn", [P, TB, 2, 6])
        bna = sb("bna", [P, TB, 2])
        mx = sb("mx", [P, 2, HG])
        den = sb("den", [P, 2, HG])
        rden = sb("rden", [P, 2, HG])
        ps = ctx.enter_context(nc.psum_tensor("ps", [P, 8, 512], F32))

        far_c, count_c, mask_c = (cst[:, i * TRI:(i + 1) * TRI] for i in range(3))
        ident, suffix, ones = (cst[:, 3 * TRI + i * P:3 * TRI + (i + 1) * P] for i in range(3))
        va_n = y_sb[:, 0, :].rearrange("p (b c) -> p b c", b=TB)
        uT = y_sb[:, 1, :].rearrange("p (f t) -> p f t", t=T)
        sgu_nat = v_sb[:, :, :].rearrange("p b (g j) -> p (b g) j", j=P)
        gain_rows = tmp[0:4 * KT, HG - 1, 0:P]
        relu_t, sq_t = qT, kT
        junk = tmp[:, 0:HG, :].rearrange("p h c -> p (h c)")
        lng_b, lnb_b = gpost[:, 0:A_W], gpost[:, A_W:D]

        def bank2(b):
            return ps[:, 2 * b:2 * b + 2, :]

        def bank2_tiles(b):
            return bank2(b).rearrange("p b (f t) -> p (b f) t", t=T)

        s_x = [sem(f"s_x{i}") for i in range(4)]
        s_id = sem("s_id")
        s_cst = sem("s_cst")
        s_rows = sem("s_rows")
        s_sguw = sem("s_sguw")
        s_sgub = sem("s_sgub")
        raw_landed = [sem(f"raw_landed{i}") for i in range(QUARTERS)]
        s_gp = sem("s_gp")
        s_out = sem("s_out")
        hi_ready = sem("hi_ready")
        lo_ready = sem("lo_ready")
        pe_ticks = sem("pe_ticks")
        post_done = sem("post_done")
        act_post = sem("act_post")
        s_tril = sem("s_tril")
        s_half = sem("s_half")
        s_mean = sem("s_mean")
        s_pow = sem("s_pow")
        s_prepT = sem("s_prepT")
        s_prep = sem("s_prep")
        s_ssx = sem("s_ssx")
        s_ssy = sem("s_ssy")
        s_yg = sem("s_yg")
        s_ysum = sem("s_ysum")
        s_xupd = sem("s_xupd")
        s_dve = sem("s_dve")
        s_xr = sem("s_xr")
        s_tr = sem("s_tr")
        s_ehi = sem("s_ehi")
        s_elo = sem("s_elo")
        s_y0 = sem("s_y0")
        f_relu, f_sq, f_hi = sem("f_relu"), sem("f_sq"), sem("f_hi")
        s_ln = sem("s_ln")
        s_mix, s_gate, s_ghi, s_glo = sem("s_mix"), sem("s_gate"), sem("s_ghi"), sem("s_glo")
        s_sgt = sem("s_sgt")
        s_sc = sem("s_sc")
        s_zs = sem("s_zs")
        s_sm = sem("s_sm")
        s_ex = sem("s_ex")
        s_pn = sem("s_pn")
        s_pT = sem("s_pT")
        s_pc = sem("s_pc")
        s_ab = sem("s_ab")
        s_sp = sem("s_sp")
        s_S = sem("s_S")
        s_e = sem("s_e")
        s_a = sem("s_a")
        s_o = sem("s_o")
        s_ohi = sem("s_ohi")
        s_olo = sem("s_olo")

        block = ctx.enter_context(nc.Block())

        @block.sync
        def _(sp):
            def load_quarter(u, q, w, k0, col):
                if not (isinstance(u, int) and u == 0):
                    sp.wait_ge(lo_ready, 8 * u + (2 * q - 6))
                src = w[bass.ds(k0 + 4 * P * q, 4 * P), bass.ds(col, NC)].rearrange("(k p) n -> p k n", p=P)
                sp.dma_start(w_raw[:, q, :, :], src).then_inc(raw_landed[q], 16)

            def load_unit(u, w, k0, col):
                for q in range(QUARTERS):
                    load_quarter(u, q, w, k0, col)

            def load_out(u0, w):
                at = 0
                for u, s in OUT_ORDER:
                    if s % 2 == 0:
                        sp.wait_ge(lo_ready, 8 * u0 + 2 * at - 6)
                        src = w[4 * P * (s // 2):4 * P * (s // 2 + 1), u * NC:(u + 1) * NC]
                        sp.dma_start(w_raw[:, at % 4, :, :], src.rearrange("(k p) n -> p k n", p=P)
                                     ).then_inc(raw_landed[at % 4], 16)
                        at += 1

            def load_gain(gain, layer, free_after):
                sp.wait_ge(post_done, free_after)
                sp.dma_start(gpost[:, :], gain[layer:layer + 1, :].partition_broadcast(P)
                             ).then_inc(s_gp, 16)

            def load_ffn(u0, layer):
                w1, w2 = ffn_w1[layer], ffn_w2[layer]
                with sp.Fori(0, FGROUPS - 1) as g:
                    with sp.Fori(0, 4) as j:
                        load_unit(u0 + 8 * g + j, w1, 0, (4 * g + j) * NC)
                    with sp.Fori(0, 4) as j:
                        load_unit(u0 + 8 * g + 4 + j, w2, g * D, j * NC)
                load_gain(post_ffn, layer, u0 + 1)
                g = FGROUPS - 1
                with sp.Fori(0, 4) as j:
                    load_unit(u0 + 8 * g + j, w1, 0, (4 * g + j) * NC)
                with sp.Fori(0, 4) as j:
                    load_unit(u0 + 8 * g + 4 + j, w2, g * D, j * NC)

            for i, (b, half) in enumerate(ROW_HALVES):
                sp.dma_start(x_sb[:, b, half], x_in[0, b * P:(b + 1) * P, half]).then_inc(s_x[i], 16)
            load_unit(0, ab_w_in[0], 0, 2 * NC)
            sp.dma_start(sgu_nat, sgu_w[0].rearrange("g i j -> i g j")).then_inc(s_sguw, 16)
            sp.dma_start(lng_b, ln_g[0:1, :].partition_broadcast(P)).then_inc(s_sgub, 16)
            sp.dma_start(lnb_b, ln_b[0:1, :].partition_broadcast(P)).then_inc(s_sgub, 16)
            load_unit(1, ab_w_in[0], 0, 3 * NC)
            sp.dma_start(sgu_bb[:, :, :].rearrange("p g i -> p (g i)"),
                         sgu_b[0:1].rearrange("o g i -> o (g i)").partition_broadcast(P)).then_inc(s_sgub, 16)
            sp.dma_start(cst[:, 0:3 * TRI], shapes[:, 0:3 * TRI]).then_inc(s_cst, 16)
            for u, c in ((2, 0), (3, 1)):
                load_unit(u, ab_w_in[0], 0, c * NC)
            with sp.Fori(0, 2) as g:
                for i in range(3):
                    load_unit(4 + 3 * g + i, ab_w_in[0], 0, (4 + 2 * i + g) * NC)
            load_gain(post_mix, 0, 5)
            load_out(U_OUT0, ab_w_out[0])
            load_ffn(U_FFN0, 0)
            with sp.Fori(0, L1_GROUPS) as g:
                for i in range(3):
                    load_unit(U_IN1 + 3 * g + i, sb_w_in[0], 0, (4 * i + g) * NC)
            load_gain(post_mix, 1, U_IN1)
            load_out(U_OUT1, sb_w_out[0])
            load_ffn(U_FFN1, 1)
            for i, (b, half) in enumerate(ROW_HALVES):
                sp.wait_ge(s_xupd, 4 * 3 + i + 1)
                sp.dma_start(out[0, b * P:(b + 1) * P, half], x_sb[:, b, half]).then_inc(s_out, 16)
            sp.wait_ge(s_out, 64)

        @block.gpsimd
        def _(pool):
            nc.gpsimd.memset(neg_half[:, :], -0.5).then_inc(s_half, 1)
            pool.wait_ge(s_half, 1)
            done = 0

            def power(cols):
                nonlocal done
                done += 1
                pool.wait_ge(s_mean, done)
                nc.gpsimd.tensor_tensor(rst[:, cols], rst[:, cols], neg_half[:, 0:cols.stop - cols.start], ALU.pow
                                        ).then_inc(s_pow, 1)

            rs_y, rs_x0, rs_x1, rs_ln = slice(2, 4), slice(6, 7), slice(7, 8), slice(8, 10)
            power(rs_x0)
            power(rs_x1)
            pool.wait_ge(s_sguw, 16)
            nc.gpsimd.affine_select(out=sgu_nat, in_=sgu_nat, compare_op=ALU.is_ge, fill=0.0, base=0,
                                    pattern=[[0, GROUPS], [-1, P]], channel_multiplier=1).then_inc(s_tril, 1)
            power(rs_ln)
            for layer in range(LAYERS):
                for cols in (rs_y, rs_x0, rs_x1):
                    power(cols)
                pool.wait_ge(s_tr, 8 * (2 * layer + 2))
                nc.gpsimd.memset(y_sb[:, :, :], 0.0).then_inc(s_y0, 1)
                for cols in (rs_y, rs_x0, rs_x1) if layer == 0 else (rs_y,):
                    power(cols)

        @block.scalar
        def _(act):
            def conv(u, t):
                act.wait_ge(raw_landed[t // 2], 16 * (u + 1))
                if not (isinstance(u, int) and 8 * u + t < RING):
                    act.wait_ge(pe_ticks, 8 * u + (t - RING + 1))
                h = 2 * (t % 2)
                nc.scalar.activation(w_hi[:, t % RING, :, :], w_raw[:, t // 2, h:h + 2, :], ACT.Copy
                                     ).then_inc(hi_ready, 1)

            def conv_at(u, t):
                if t < 4:
                    conv(u, t + 4)
                elif not (isinstance(u, int) and u == UNITS - 1):
                    conv(u + 1, t - 4)

            def unit(u, post, extras=None):
                for t in range(1, TICKS):
                    for f in (extras or {}).get(t, []):
                        f()
                    conv_at(u, t)
                post()
                if not (isinstance(u, int) and u == UNITS - 1):
                    conv(u + 1, 4)

            def unit_finished(u):
                act.wait_ge(pe_ticks, 8 * u + 8)

            def nothing():
                pass

            def evacuate(k):
                for j in range(8):
                    act.wait_ge(s_tr, 8 * k + j + 1)
                    b = 2 + j if j < 6 else j - 4
                    for i in range(2):
                        kt = 2 * j + i
                        last = nc.scalar.activation(act_hi[:, kt, :], ps[:, b, i * T:(i + 1) * T], ACT.Copy,
                                                    scale=gpre[:, k * KT + kt:k * KT + kt + 1])
                    last.then_inc(s_ehi, 1)

            squares = [0, 0]

            def junk_free():
                for semaphore, n in zip((s_ssx, s_ssy), squares):
                    if n:
                        act.wait_ge(semaphore, n)

            def squares_x_half(k, i):
                b, half = ROW_HALVES[i]
                if k:
                    act.wait_ge(s_xupd, 4 * (k - 1) + i + 1)
                else:
                    act.wait_ge(s_x[i], 16)
                junk_free()
                squares[0] += 1
                nc.scalar.activation(junk[:, 0:D // 2], x_sb[:, b, half], ACT.Square,
                                     accum_out=ssx[:, b, i % 2:i % 2 + 1]).then_inc(s_ssx, 1)

            def transition(k):
                for i in range(4):
                    squares_x_half(k, i)
                evacuate(k)

            def l0_exp(grp):
                act.wait_ge(s_sm, 4 * grp + 4)
                nc.scalar.activation(zs[:, :, :], zs[:, :, :], ACT.Exp).then_inc(s_ex, 1)

            def l0_copy_pT(n):
                act.wait_ge(s_pT, n + 1)
                b = 2 * (n % 2)
                nc.scalar.activation(tmp[:, b:b + 2, :], ps[:, 6:8, 0:TRI], ACT.Copy).then_inc(s_pc, 1)

            def o_hi(n, b, tile):
                act.wait_ge(s_o, n + 1)
                nc.scalar.activation(hid_hi[:, bass.ds(tile, 2), :],
                                     ps[:, 6 + b, :].rearrange("p (h t) -> p h t", t=T), ACT.Copy).then_inc(s_ohi, 1)

            def l0_extras(grp):
                return {9: [lambda: l0_exp(grp)], 13: [lambda: l0_copy_pT(2 * grp)],
                        14: [lambda: l0_copy_pT(2 * grp + 1)],
                        15: [lambda: o_hi(2 * grp, 0, 8 + 4 * grp)],
                        17: [lambda: o_hi(2 * grp + 1, 1, 8 + 4 * grp + 2)]}

            def l1_logs(b, grp):
                pair = 2 * grp + b
                z, t = zs[:, 2 * b:2 * b + 2, :], tmp[:, 0:2, :]
                act.wait_ge(s_zs, 4 * grp + (8 + 2 * b + 2))
                if b == 1:
                    act.wait_ge(s_sp, pair)
                nc.scalar.activation(t, z, ACT.Abs).then_inc(s_ab, 1)
                act.wait_ge(s_ab, 3 * pair + 1)
                nc.scalar.activation(t, t, ACT.Exp, scale=-1.0).then_inc(s_ab, 1)
                act.wait_ge(s_ab, 3 * pair + 2)
                nc.scalar.activation(t, t, ACT.Ln, bias=1.0).then_inc(s_ab, 1)

            def l1_weights(b, grp):
                z = zs[:, 2 * b:2 * b + 2, :]
                act.wait_ge(s_e, 2 * grp + (b + 1))
                nc.scalar.activation(z, z, ACT.Exp).then_inc(s_a, 1)

            def l1_extras(grp):
                return {4: [lambda: l1_logs(0, grp)], 6: [lambda: l1_logs(1, grp)],
                        9: [lambda: l1_weights(0, grp)], 10: [lambda: o_hi(2 * grp + 4, 0, 4 * grp)],
                        13: [lambda: l1_weights(1, grp)], 14: [lambda: o_hi(2 * grp + 5, 1, 4 * grp + 2)]}

            def qkv_group(u, extras):
                for i in range(3):
                    unit(u + i, nothing, {t - 8 * i: f for t, f in extras.items() if 8 * i < t < 8 * i + 8})

            def sum_squares_y(src, c):
                for b in range(TB):
                    junk_free()
                    squares[1] += 1
                    nc.scalar.activation(junk[:, 2 * NC:3 * NC], src[b], ACT.Square, accum_out=ssy[:, b, c:c + 1]
                                         ).then_inc(s_ssy, 1)

            def sum_squares_psum(u0, c):
                for b in range(TB):
                    junk_free()
                    if b:
                        act.wait_ge(s_yg, 8 * (u0 == U_OUT1) + 2 * c + 1)
                    squares[1] += 1
                    nc.scalar.activation(junk[:, 2 * NC:3 * NC], ps[:, 2 * OUT_BUF[c] + b, :], ACT.Square,
                                         accum_out=ssy[:, b, c:c + 1]).then_inc(s_ssy, 1)

            def out_phase(u0, extras, first_post):
                for t in range(1, 32):
                    for f in extras.get(t, []):
                        f()
                    if t in OUT_POST:
                        c = OUT_POST[t]
                        act.wait_ge(pe_ticks, 8 * u0 + t)
                        sum_squares_psum(u0, c)
                    conv_at(u0 + t // 8, t % 8)
                unit_finished(u0 + 3)
                sum_squares_psum(u0, 3)

            def ffn(u0, layer):
                f0 = 16 * layer

                def up(g, jj, par):
                    u, f = u0 + 8 * g + 2 * jj + par, f0 + 4 * g + 2 * jj + par

                    def post():
                        unit_finished(u)
                        nc.scalar.activation(relu_t[:, :, :], bank2_tiles(par), ACT.Relu).then_inc(f_relu, 1)
                        act.wait_ge(f_sq, f + 1)
                        nc.scalar.activation(hid_hi[:, bass.ds(8 * jj + 4 * par, 4), :], sq_t[:, :, :], ACT.Copy
                                             ).then_inc(f_hi, 1)
                    unit(u, post)

                def group_up(g):
                    with act.Fori(0, 2) as jj:
                        for par in range(2):
                            up(g, jj, par)

                with act.Fori(0, FGROUPS - 1) as g:
                    group_up(g)
                    with act.Fori(0, 2) as jj:
                        for par in range(2):
                            unit(u0 + 8 * g + 4 + 2 * jj + par, nothing)
                group_up(FGROUPS - 1)
                for j in range(4):
                    u = u0 + 8 * (FGROUPS - 1) + 4 + j

                    def post(j=j):
                        act.wait_ge(s_ysum, 4 * layer + j + 1)
                        sum_squares_y([junk[:, b * NC:(b + 1) * NC] for b in range(TB)], j)
                        if j == 3:
                            after_ffn(layer)
                    unit(u, post)

            def after_ffn(layer):
                if layer == 0:
                    transition(2)

            act.dma_start(cst[:, 3 * TRI:], shapes[:, 3 * TRI:]).then_inc(s_id, 16)
            for i, (g, l) in enumerate(((pre_mix, 0), (pre_ffn, 0), (pre_mix, 1), (pre_ffn, 1))):
                act.dma_start(tmp[i * KT:(i + 1) * KT, HG - 1, 0:P], g[l].rearrange("(k p) -> k p", p=P)
                              ).then_inc(s_rows, 16)
            for i in range(2):
                squares_x_half(0, i)
            act.wait_ge(s_prepT, 1)
            nc.scalar.activation(gpre[:, :], ps[:, 0, 0:4 * KT], ACT.Copy).then_inc(s_prep, 1)
            for t in range(4):
                conv(0, t)
            act.wait_ge(s_prep, 1)
            evacuate(0)
            conv(0, 4)

            def gelu_v(j):
                unit_finished(j)
                nc.scalar.activation(va_n[:, :, j * NC:(j + 1) * NC], bank2(j), ACT.Gelu).then_inc(act_post, 1)

            def gelu_u(j):
                unit_finished(2 + j)
                nc.scalar.activation(uT[:, 4 * j:4 * j + 4, :], bank2_tiles(j), ACT.Gelu).then_inc(act_post, 1)

            def gate_hi(m):
                act.wait_ge(s_gate, m + 1)
                nc.scalar.activation(hid_hi[:, 2 * m:2 * m + 2, :],
                                     gated, ACT.Copy
                                     ).then_inc(s_ghi, 1)

            gated = junk[:, 512:1024].rearrange("p (g t) -> p g t", t=T)
            def sgu_weights():
                act.wait_ge(s_prepT, 3)
                nc.scalar.activation(sgu_wT[:, :, :], ps[:, 6:8, :].rearrange("p b (g i) -> p (b g) i", i=P), ACT.Copy
                                     ).then_inc(s_prep, 1)

            unit(0, lambda: gelu_v(0))
            unit(1, lambda: gelu_v(1), {6: [sgu_weights]})
            for j in range(2):
                unit(2 + j, lambda j=j: gelu_u(j))
            qkv_group(4, {m + 1: [lambda m=m: gate_hi(m)] for m in range(4)})
            qkv_group(7, l0_extras(0))
            out_phase(U_OUT0, l0_extras(1), None)
            transition(1)
            conv(U_FFN0, 4)
            ffn(U_FFN0, 0)

            qkv_group(U_IN1, {})
            with act.Fori(1, L1_GROUPS) as g:
                qkv_group(U_IN1 + 3 * g, l1_extras(g - 1))
            out_phase(U_OUT1, l1_extras(L1_GROUPS - 1), None)
            transition(3)
            conv(U_FFN1, 4)
            ffn(U_FFN1, 1)

        @block.vector
        def _(dve):
            steps, powers = [0], [0]

            def chain(ins):
                steps[0] += 1
                ins.then_inc(s_dve, 1)
                dve.wait_ge(s_dve, steps[0])

            def conv(u, t):
                dve.wait_ge(hi_ready, 8 * u + (t + 1))
                h = 2 * (t % 2)
                nc.vector.tensor_tensor(w_lo[:, t % RING, :, :], w_raw[:, t // 2, h:h + 2, :],
                                        w_hi[:, t % RING, :, :].bitcast(F32), ALU.subtract).then_inc(lo_ready, 1)

            def conv_at(u, t):
                if t < 4:
                    conv(u, t + 4)
                elif not (isinstance(u, int) and u == UNITS - 1):
                    conv(u + 1, t - 4)

            def unit(u, post, extras=None):
                for t in range(1, TICKS):
                    for f in (extras or {}).get(t, []):
                        f()
                    conv_at(u, t)
                post()
                if not (isinstance(u, int) and u == UNITS - 1):
                    conv(u + 1, 4)

            def unit_finished(u):
                dve.wait_ge(pe_ticks, 8 * u + 8)

            def rsqrt(dst, src, scale, eps):
                nc.vector.tensor_scalar(dst, src, scale, eps, ALU.mult, ALU.add).then_inc(s_mean, 1)
                powers[0] += 1
                dve.wait_ge(s_pow, powers[0])

            def update_x(k):
                dve.wait_ge(s_ssy, 8 * k)
                chain(nc.vector.tensor_reduce(rst[:, 0:2], ssy[:, :, :], AX.X, ALU.add))
                rsqrt(rst[:, 2:4], rst[:, 0:2], 1.0 / D, RMS_EPS)
                for b, half in ROW_HALVES:
                    xs = x_sb[:, b, half]
                    nc.vector.scalar_tensor_tensor(xs, y_sb[:, b, half], rst[:, 2 + b:3 + b], xs,
                                                   ALU.mult, ALU.add).then_inc(s_xupd, 1)

            def normed_rows(k):
                for b in range(TB):
                    if k or b == 0:
                        dve.wait_ge(s_ssx, max(4 * k - 2, 0) + 2 * b + 2)
                    chain(nc.vector.tensor_reduce(rst[:, 4 + b:5 + b], ssx[:, b, :], AX.X, ALU.add))
                    rsqrt(rst[:, 6 + b:7 + b], rst[:, 4 + b:5 + b], 1.0 / D, RMS_EPS)
                    if k:
                        dve.wait_ge(s_xupd, 4 * (k - 1) + 2 * b + 2)
                    elif b == 0:
                        for i in range(2):
                            dve.wait_ge(s_x[i], 16)
                    nc.vector.tensor_scalar(y_sb[:, b, :], x_sb[:, b, :], rst[:, 6 + b:7 + b], None, ALU.mult
                                            ).then_inc(s_xr, 1)

            def evacuate(k):
                for j in range(8):
                    dve.wait_ge(s_ehi, 8 * k + j + 1)
                    b = 2 + j if j < 6 else j - 4
                    for i in range(2):
                        kt = 2 * j + i
                        last = nc.vector.scalar_tensor_tensor(
                            act_lo[:, kt, :], ps[:, b, i * T:(i + 1) * T], gpre[:, k * KT + kt:k * KT + kt + 1],
                            act_hi[:, kt, :].bitcast(F32), ALU.mult, ALU.subtract)
                    last.then_inc(s_elo, 1)

            def transition(k):
                update_x(k)
                normed_rows(k)
                evacuate(k)

            def l0_scores(h, head):
                dve.wait_ge(s_sc, head + 1)
                dve.wait_ge(s_cst, 16)
                nc.vector.scalar_tensor_tensor(zs[:, h, :], far_c, -(2.0 ** -(head + 1)), ps[:, 6 + h % 2, 0:TRI],
                                               ALU.mult, ALU.add).then_inc(s_zs, 1)

            def halves(t):
                return t[:, :, 0:P], t[:, :, P:TRI]

            def l0_max(grp):
                dve.wait_ge(s_zs, 4 * grp + 4)
                for i, z in enumerate(halves(zs)):
                    nc.vector.tensor_reduce(mx[:, i, :], z, AX.X, ALU.max).then_inc(s_sm, 1)

            def l0_less_max(grp):
                dve.wait_ge(s_sm, 4 * grp + 2)
                for i, z in enumerate(halves(zs)):
                    m = mx[:, i, :].unsqueeze(2).broadcast_to([P, HG, z.shape[2]])
                    nc.vector.tensor_tensor(z, z, m, ALU.subtract).then_inc(s_sm, 1)

            def l0_count(grp):
                dve.wait_ge(s_ex, grp + 1)
                chain(nc.vector.tensor_tensor(zs[:, :, :], zs[:, :, :],
                                              count_c.unsqueeze(1).broadcast_to([P, HG, TRI]), ALU.mult))

            def l0_normalise(grp):
                for i, z in enumerate(halves(zs)):
                    chain(nc.vector.tensor_reduce(den[:, i, :], z, AX.X, ALU.add))
                chain(nc.vector.reciprocal(rden[:, :, :], den[:, :, :]))
                for i, z in enumerate(halves(zs)):
                    m = rden[:, i, :].unsqueeze(2).broadcast_to([P, HG, z.shape[2]])
                    nc.vector.tensor_tensor(z, z, m, ALU.mult).then_inc(s_pn, 1)

            def o_lo(n, b, tile):
                dve.wait_ge(s_ohi, n + 1)
                nc.vector.tensor_tensor(hid_lo[:, bass.ds(tile, 2), :], ps[:, 6 + b, :].rearrange("p (h t) -> p h t", t=T),
                                        hid_hi[:, bass.ds(tile, 2), :].bitcast(F32), ALU.subtract).then_inc(s_olo, 1)

            def l0_extras(grp):
                e = {2 + h: [lambda h=h: l0_scores(h, 4 * grp + h)] for h in range(4)}
                e.update({6: [lambda: l0_max(grp)], 7: [lambda: l0_less_max(grp)], 9: [lambda: l0_count(grp)],
                          10: [lambda: l0_normalise(grp)], 15: [lambda: o_lo(2 * grp, 0, 8 + 4 * grp)],
                          17: [lambda: o_lo(2 * grp + 1, 1, 8 + 4 * grp + 2)]})
                return e

            def l1_scores(h, grp):
                dve.wait_ge(s_sc, 4 * grp + (8 + h + 1))
                nc.vector.tensor_tensor(zs[:, h, :], ps[:, 6 + h % 2, 0:TRI], mask_c, ALU.add).then_inc(s_zs, 1)

            def l1_softplus(b, grp):
                dve.wait_ge(s_ab, 6 * grp + 3 * b + 3)
                nc.vector.scalar_tensor_tensor(tmp[:, 2:4, :], zs[:, 2 * b:2 * b + 2, :], 0.0, tmp[:, 0:2, :],
                                               ALU.max, ALU.add).then_inc(s_sp, 1)

            def l1_exponent(b, grp):
                dve.wait_ge(s_S, 2 * grp + (b + 1))
                z = zs[:, 2 * b:2 * b + 2, :]
                nc.vector.tensor_tensor(z, z, ps[:, 6:8, 0:TRI], ALU.add).then_inc(s_e, 1)

            def l1_extras(grp):
                e = {2 + h: [lambda h=h: l1_scores(h, grp)] for h in range(4)}
                e[5].append(lambda: l1_softplus(0, grp))
                e.update({7: [lambda: l1_exponent(0, grp)], 9: [lambda: l1_softplus(1, grp)],
                          10: [lambda: o_lo(2 * grp + 4, 0, 4 * grp)], 12: [lambda: l1_exponent(1, grp)],
                          14: [lambda: o_lo(2 * grp + 5, 1, 4 * grp + 2)]})
                return e

            def qkv_group(u, extras):
                def post_q():
                    unit_finished(u)
                    nc.vector.tensor_scalar(qT[:, :, :], bank2_tiles(0), SCALE, None, ALU.mult).then_inc(post_done, 1)

                def post_k():
                    unit_finished(u + 1)
                    nc.vector.tensor_copy(kT[:, :, :], bank2_tiles(1)).then_inc(post_done, 1)

                def post_v():
                    unit_finished(u + 2)
                    nc.vector.tensor_copy(v_sb[:, :, :], bank2(2)).then_inc(post_done, 1)

                for i, post in enumerate((post_q, post_k, post_v)):
                    unit(u + i, post, {t - 8 * i: f for t, f in extras.items() if 8 * i < t < 8 * i + 8})

            def out_phase(u0, extras, k):
                def post(c, t):
                    dve.wait_ge(pe_ticks, 8 * u0 + t)
                    dve.wait_ge(s_gp, 16 * k)
                    cols = slice(c * NC, (c + 1) * NC)
                    for b in (1, 0):
                        if b == 0:
                            dve.wait_ge(s_ssy, 8 * (k - 1) + 2 * c + 1)
                        ins = nc.vector.tensor_tensor(y_sb[:, b, cols], ps[:, 2 * OUT_BUF[c] + b, :], gpost[:, cols],
                                                      ALU.mult)
                        ins.then_inc(s_yg, 1)
                    dve.wait_ge(s_ssy, 8 * (k - 1) + 2 * c + 2)
                    dve.wait_ge(s_yg, 8 * (k // 2) + 2 * c + 2)
                    dve.sem_inc(post_done, 1)

                for t in range(1, 32):
                    for f in extras.get(t, []):
                        f()
                    if t in OUT_POST:
                        post(OUT_POST[t], t)
                    conv_at(u0 + t // 8, t % 8)
                post(3, 32)

            def ffn(u0, layer):
                f0 = 16 * layer

                def up(g, jj, par):
                    u, f = u0 + 8 * g + 2 * jj + par, f0 + 4 * g + 2 * jj + par

                    def post():
                        dve.wait_ge(f_relu, f + 1)
                        nc.vector.scalar_tensor_tensor(sq_t[:, :, :], bank2_tiles(par), 0.0, relu_t[:, :, :],
                                                       ALU.max, ALU.mult).then_inc(f_sq, 1)
                        dve.wait_ge(f_hi, f + 1)
                        tiles = bass.ds(8 * jj + 4 * par, 4)
                        nc.vector.tensor_tensor(hid_lo[:, tiles, :], sq_t[:, :, :], hid_hi[:, tiles, :].bitcast(F32),
                                                ALU.subtract).then_inc(post_done, 1)
                    unit(u, post)

                def group_up(g):
                    with dve.Fori(0, 2) as jj:
                        for par in range(2):
                            up(g, jj, par)

                def add_y(u, chunk, par, dst=None):
                    unit_finished(u)
                    dve.wait_ge(post_done, u)
                    ys = y_sb[:, :, bass.ds(chunk, NC)]
                    return nc.vector.tensor_tensor(ys if dst is None else dst, ys, bank2(par), ALU.add)

                with dve.Fori(0, FGROUPS - 1) as g:
                    group_up(g)
                    dve.wait_ge(s_y0, layer + 1)
                    with dve.Fori(0, 2) as jj:
                        for par in range(2):
                            u = u0 + 8 * g + 4 + 2 * jj + par
                            unit(u, lambda: add_y(u, 2 * NC * jj + NC * par, par).then_inc(post_done, 1))
                group_up(FGROUPS - 1)
                for j in range(4):
                    u = u0 + 8 * (FGROUPS - 1) + 4 + j

                    def post(j=j, u=u):
                        k = 2 * layer + 2
                        total = junk[:, 0:2 * NC].rearrange("p (b c) -> p b c", b=TB)
                        if j:
                            dve.wait_ge(s_ssy, 8 * (k - 1) + 2 * j)
                        add_y(u, j * NC, j % 2, total).then_inc(s_ysum, 1)
                        dve.wait_ge(s_ysum, 4 * layer + j + 1)
                        dve.wait_ge(s_gp, 16 * k)
                        g = gpost[:, j * NC:(j + 1) * NC].unsqueeze(1).broadcast_to([P, TB, NC])
                        nc.vector.tensor_tensor(y_sb[:, :, j * NC:(j + 1) * NC], total, g, ALU.mult
                                                ).then_inc(post_done, 1)
                        if j == 3:
                            dve.wait_ge(post_done, u + 1)
                            if layer == 0:
                                transition(2)
                            else:
                                update_x(4)
                    unit(u, post)

            for i in (2, 3):
                b, half = ROW_HALVES[i]
                dve.wait_ge(s_x[i], 16)
                chain(nc.vector.tensor_tensor_reduce(y_sb[:, b, half], x_sb[:, b, half], x_sb[:, b, half], 1.0, 0.0,
                                                     ALU.mult, ALU.add, ssx[:, b, i - 2:i - 1]))
            normed_rows(0)
            for t in range(4):
                conv(0, t)
            evacuate(0)
            conv(0, 4)

            def stats_v(j):
                dve.wait_ge(act_post, j + 1)
                for b in range(TB):
                    last = nc.vector.bn_stats(bn[:, b, j, :], va_n[:, b, j * NC:(j + 1) * NC])
                last.then_inc(post_done, 1)

            def layernorm_v(step):
                if step == 0:
                    dve.wait_ge(post_done, 2)
                    for b in range(TB):
                        chain(nc.vector.bn_aggr(bna[:, b, :], bn[:, b, :, :]))
                    rsqrt(rst[:, 8:10], bna[:, :, 1], 1.0, LN_EPS)
                    for b in range(TB):
                        nc.vector.tensor_scalar(va_n[:, b, :], va_n[:, b, :], bna[:, b, 0:1], rst[:, 8 + b:9 + b],
                                                ALU.subtract, ALU.mult).then_inc(s_ln, 1)
                else:
                    dve.wait_ge(s_ln, step + 1)
                    dve.wait_ge(s_sgub, 48)
                    g = (lng_b if step == 1 else lnb_b).unsqueeze(1).broadcast_to([P, TB, A_W])
                    nc.vector.tensor_tensor(va_n, va_n, g, ALU.mult if step == 1 else ALU.add).then_inc(s_ln, 1)

            def post_u(j):
                dve.wait_ge(act_post, 3 + j)
                dve.sem_inc(post_done, 1)

            mixed = junk[:, 0:512].rearrange("p (g c i) -> p g c i", g=2, i=P)
            gated = junk[:, 512:1024].rearrange("p (g t) -> p g t", t=T)

            def gate(m):
                dve.wait_ge(s_mix, m + 1)
                dve.wait_ge(act_post, 4)
                bias = sgu_bb[:, 2 * m:2 * m + 2, :].unsqueeze(2).broadcast_to([P, 2, TB, P])
                nc.vector.tensor_tensor(mixed, ps[:, 6 + m % 2, :].rearrange("p (g c i) -> p g c i", g=2, i=P), bias,
                                        ALU.add).then_inc(s_sgt, 1)
                dve.wait_ge(s_sgt, m + 1)
                nc.vector.tensor_tensor(gated, junk[:, 0:512].rearrange("p (g t) -> p g t", t=T),
                                        uT[:, 2 * m:2 * m + 2, :], ALU.mult).then_inc(s_gate, 1)

            def gate_lo(m):
                dve.wait_ge(s_ghi, m + 1)
                nc.vector.tensor_tensor(hid_lo[:, 2 * m:2 * m + 2, :], gated,
                                        hid_hi[:, 2 * m:2 * m + 2, :].bitcast(F32), ALU.subtract).then_inc(s_glo, 1)

            for j in range(2):
                unit(j, lambda j=j: stats_v(j))
            unit(2, lambda: post_u(0), {1 + i: [lambda i=i: layernorm_v(i)] for i in range(3)})
            unit(3, lambda: post_u(1))
            gates = {1: [lambda: gate(0)], 5: [lambda: gate_lo(3)]}
            for m in range(1, 4):
                gates[1 + m] = [lambda m=m: gate_lo(m - 1), lambda m=m: gate(m)]
            qkv_group(4, gates)
            qkv_group(7, l0_extras(0))
            out_phase(U_OUT0, l0_extras(1), 1)
            transition(1)
            conv(U_FFN0, 4)
            ffn(U_FFN0, 0)

            qkv_group(U_IN1, {})
            with dve.Fori(1, L1_GROUPS) as g:
                qkv_group(U_IN1 + 3 * g, l1_extras(g - 1))
            out_phase(U_OUT1, l1_extras(L1_GROUPS - 1), 3)
            transition(3)
            conv(U_FFN1, 4)
            ffn(U_FFN1, 1)

        @block.tensor
        def _(pe):
            def mm(dst, lhsT, rhs, start, stop):
                return nc.tensor.matmul(dst, lhsT, rhs, start=start, stop=stop, skip_group_check=True)

            def tick_tokens(buf, s, slot, hi, lo, ready):
                pe.wait_ge(lo_ready, ready)
                for i in range(2):
                    kt = 2 * s + i
                    for b in range(TB):
                        dst, tok = ps[:, 2 * buf + b, :], slice(b * P, (b + 1) * P)
                        mm(dst, hi[:, kt, tok], w_hi[:, slot, i, :], kt == 0, False)
                        mm(dst, hi[:, kt, tok], w_lo[:, slot, i, :], False, False)
                        last = mm(dst, lo[:, kt, tok], w_hi[:, slot, i, :], False, kt == KT - 1)
                last.then_inc(pe_ticks, 1)

            def tick_features(buf, s, slot, hi, lo, ready):
                pe.wait_ge(lo_ready, ready)
                for i in range(2):
                    kt = 2 * s + i
                    for f in range(4):
                        dst, cols = ps[:, 2 * buf + f // 2, (f % 2) * T:(f % 2 + 1) * T], slice(f * P, (f + 1) * P)
                        mm(dst, w_hi[:, slot, i, cols], hi[:, kt, :], kt == 0 and f % 2 == 0, False)
                        mm(dst, w_hi[:, slot, i, cols], lo[:, kt, :], False, False)
                        last = mm(dst, w_lo[:, slot, i, cols], hi[:, kt, :], False, kt == KT - 1)
                last.then_inc(pe_ticks, 1)

            def unit(u, tick, buf, hi=act_hi, lo=act_lo, fresh=None, extras=None, before=None, posts=None):
                need = u if fresh is not None or posts == "all" else u - 1
                if not (isinstance(need, int) and need <= 0):
                    pe.wait_ge(post_done, need)
                for s in range(TICKS):
                    for f in (extras or {}).get(s, []):
                        f()
                    if fresh is not None:
                        pe.wait_ge(s_elo, 8 * fresh + s + 1)
                    if before is not None:
                        before(s)
                    tick(buf, s, s % RING, hi, lo, 8 * u + (s + 1))

            def transposes(k, u):
                if u:
                    pe.wait_ge(post_done, u)

                def half(j, b):
                    bank = 2 + j if j < 6 else j - 4
                    for i in range(2):
                        kt = 2 * j + i
                        last = nc.tensor.transpose(ps[:, bank, i * T + b * P:i * T + (b + 1) * P],
                                                   y_sb[:, b, kt * P:(kt + 1) * P], ident)
                    return last

                for b in range(TB):
                    pe.wait_ge(s_xr, 2 * k + b + 1)
                    for j in range(6):
                        last = half(j, b)
                        if b == 1:
                            last.then_inc(s_tr, 1)
                for j in (6, 7):
                    pe.wait_ge(s_elo, 8 * k + j - 5)
                    half(j, 0)
                    half(j, 1).then_inc(s_tr, 1)

            def l0_scores(h, head):
                if h >= 2:
                    pe.wait_ge(s_zs, head - 1)
                if h == 0:
                    pe.wait_ge(post_done, 7 + 3 * (head // 4))
                b = 6 + h % 2
                mm(ps[:, b, 0:P], qT[:, h, 0:P], kT[:, h, 0:P], True, True)
                mm(ps[:, b, P:TRI], qT[:, h, P:T], kT[:, h, :], True, True).then_inc(s_sc, 1)

            def l0_pT(n):
                if n % 2 == 0:
                    pe.wait_ge(s_pn, n + 2)
                else:
                    pe.wait_ge(s_pc, n)
                for i in range(2):
                    for c in range(3):
                        last = nc.tensor.transpose(ps[:, 6 + i, c * P:(c + 1) * P],
                                                   zs[:, 2 * (n % 2) + i, c * P:(c + 1) * P], ident)
                last.then_inc(s_pT, 1)

            def values(b, w):
                for i in range(2):
                    vh = slice((2 * b + i) * P, (2 * b + i + 1) * P)
                    mm(ps[:, 6 + b, i * T:(i + 1) * T], v_sb[:, 0, vh], w[:, i, 0:T], i == 0, False)
                    last = mm(ps[:, 6 + b, i * T + P:(i + 1) * T], v_sb[:, 1, vh], w[:, i, T:TRI], False, True)
                last.then_inc(s_o, 1)

            def l0_values(n, b):
                pe.wait_ge(s_pc, n - n % 2 + 2)
                values(b, tmp[:, 2 * b:2 * b + 2, :])

            def l0_extras(grp):
                e = {2 + h: [lambda h=h: l0_scores(h, 4 * grp + h)] for h in range(4)}
                e.update({13: [lambda: l0_pT(2 * grp)], 14: [lambda: l0_pT(2 * grp + 1)],
                          15: [lambda: l0_values(2 * grp, 0)], 16: [lambda: l0_values(2 * grp + 1, 1)]})
                return e

            def l1_scores(h, grp):
                if h >= 2:
                    pe.wait_ge(s_zs, 4 * grp + (8 + h - 1))
                if h == 0:
                    pe.wait_ge(post_done, 3 * grp + (U_IN1 + 3))
                    pe.wait_ge(s_olo, 2 * grp + 4)
                b = 6 + h % 2
                mm(ps[:, b, 0:T], kT[:, h, 0:P], qT[:, h, :], True, True)
                mm(ps[:, b, T:TRI], kT[:, h, P:T], qT[:, h, P:T], True, True).then_inc(s_sc, 1)

            def l1_suffix(b, grp):
                pe.wait_ge(s_sp, 2 * grp + (b + 1))
                pe.wait_ge(s_zs, 4 * grp + (8 + 4))
                if b == 1:
                    pe.wait_ge(s_olo, 2 * grp + 5)
                for i in range(2):
                    z, dst = tmp[:, 2 + i, :], ps[:, 6 + i, :]
                    mm(dst[:, 0:T], suffix, z[:, 0:T], True, False)
                    mm(dst[:, P:T], ones, z[:, T:TRI], False, True)
                    last = mm(dst[:, T:TRI], suffix, z[:, T:TRI], False, True)
                last.then_inc(s_S, 1)

            def l1_values(b, grp):
                pe.wait_ge(s_a, 2 * grp + (b + 1))
                values(b, zs[:, 2 * b:2 * b + 2, :])

            def l1_extras(grp):
                e = {2 + h: [lambda h=h: l1_scores(h, grp)] for h in range(4)}
                e.update({7: [lambda: l1_suffix(0, grp)], 10: [lambda: l1_values(0, grp)],
                          12: [lambda: l1_suffix(1, grp)], 14: [lambda: l1_values(1, grp)]})
                return e

            def qkv_group(u, extras, fresh=None):
                for i, tick in enumerate((tick_features, tick_features, tick_tokens)):
                    unit(u + i, tick, i, fresh=fresh if i == 0 else None,
                         extras={t - 8 * i: f for t, f in extras.items() if 8 * i <= t < 8 * i + 8})

            def out_phase(u0, extras, ready):
                for t, (u, s) in enumerate(OUT_ORDER):
                    for f in extras.get(t, []):
                        f()
                    if s == 0:
                        pe.wait_ge(post_done, u0 + (1 if u == 3 else 0 if u == 2 else -1))
                    if t < 6 or t in (18, 19):
                        for semaphore, value in ready(s):
                            pe.wait_ge(semaphore, value)
                    tick_tokens(OUT_BUF[u], s, t % RING, hid_hi, hid_lo, 8 * u0 + t + 1)

            def ffn(u0, k):
                def up(g, first):
                    with pe.Fori(0, 2) as jj:
                        for par in range(2):
                            unit(u0 + 8 * g + 2 * jj + par, tick_features, par)

                def down(g):
                    def hidden_ready(s):
                        if s % 2 == 0:
                            pe.wait_ge(post_done, u0 + 8 * g + (s // 2 + 1))

                    with pe.Fori(0, 2) as jj:
                        for par in range(2):
                            unit(u0 + 8 * g + 4 + 2 * jj + par, tick_tokens, par, hid_hi, hid_lo,
                                 before=hidden_ready)

                unit(u0, tick_features, 0, fresh=k)
                unit(u0 + 1, tick_features, 1)
                for par in range(2):
                    unit(u0 + 2 + par, tick_features, par)
                down(0)
                with pe.Fori(1, FGROUPS) as g:
                    up(g, False)
                    down(g)

            pe.wait_ge(s_id, 16)
            pe.wait_ge(s_rows, 64)
            nc.tensor.transpose(ps[:, 0, 0:4 * KT], gain_rows, ident[0:4 * KT, 0:4 * KT]).then_inc(s_prepT, 1)
            transposes(0, 0)

            def sgu_weights():
                pe.wait_ge(s_tril, 1)
                for g in range(GROUPS):
                    last = nc.tensor.transpose(ps[:, 6 + g // 4, (g % 4) * P:(g % 4 + 1) * P], sgu_nat[:, g, :], ident)
                    if g % 4 == 3:
                        last.then_inc(s_prepT, 1)

            def mix(m):
                if m == 0:
                    pe.wait_ge(s_prep, 2)
                    pe.wait_ge(s_ln, 4)
                if m >= 2:
                    pe.wait_ge(s_sgt, m - 1)
                for i in range(2):
                    g = 2 * m + i
                    for c in range(TB):
                        last = mm(ps[:, 6 + m % 2, i * T + c * P:i * T + (c + 1) * P],
                                  va_n[:, c, g * P:(g + 1) * P], sgu_wT[:, g, :], True, True)
                last.then_inc(s_mix, 1)

            pe.wait_ge(s_prep, 1)
            unit(0, tick_tokens, 0, fresh=0)
            unit(1, tick_tokens, 1, extras={5: [sgu_weights]})
            unit(2, tick_features, 0)
            unit(3, tick_features, 1)
            qkv_group(4, {1 + m: [lambda m=m: mix(m)] for m in range(4)})
            qkv_group(7, l0_extras(0))

            def ready0(s):
                if s < 4:
                    return [(s_glo, s + 1)]
                return [(s_olo, s - 3)]
            out_phase(U_OUT0, l0_extras(1), ready0)
            transposes(1, U_FFN0)
            ffn(U_FFN0, 1)

            transposes(2, U_IN1)
            qkv_group(U_IN1, {}, fresh=2)
            with pe.Fori(1, L1_GROUPS) as g:
                qkv_group(U_IN1 + 3 * g, l1_extras(g - 1))
            out_phase(U_OUT1, l1_extras(L1_GROUPS - 1), lambda s: [(s_olo, 4 + s + 1)])
            transposes(3, U_FFN1)
            ffn(U_FFN1, 3)


_INS = ['x', 'norm_pre_mix', 'norm_post_mix', 'norm_pre_ffn', 'norm_post_ffn', 'ab_w_in', 'sgu_ln_g', 'sgu_ln_b',
        'sgu_w', 'sgu_b', 'ab_w_out', 'sb_w_in', 'sb_w_out', 'ffn_w1', 'ffn_w2']
_OUT = ((1, T, D), 'float32')


def kernel(**inputs):
    import numpy as _np
    import concourse.bacc as _bacc
    from concourse import mybir as _mybir
    from concourse.bass_utils import run_bass_kernel_spmd as _run

    nc = _bacc.Bacc("TRN2", target_bir_lowering=False, num_devices=1)
    arrays, args = {}, []
    for name in _INS:
        arrays[f"in_{name}_dram"] = _np.ascontiguousarray(inputs[name])
    arrays["shape_constants_dram"] = shape_constants()
    for name, a in arrays.items():
        args.append(nc.dram_tensor(name, a.shape, _mybir.dt.from_np(a.dtype), kind="ExternalInput").ap())
    args.append(nc.dram_tensor("out_dram", _OUT[0], _mybir.dt.from_np(_np.dtype(_OUT[1])), kind="ExternalOutput").ap())
    trunk_kernel(nc, *args)
    r = _run(nc, [arrays], core_ids=[0])
    return r.results[0]["out_dram"]
```

```python
from contextlib import ExitStack

import numpy as np

import concourse.bass as bass
from concourse import mybir

F32 = mybir.dt.float32
F32R = mybir.dt.float32r
ALU = mybir.AluOpType
ACT = mybir.ActivationFunctionType
AX = mybir.AxisListType

P = 128
T = 256
TB = T // P
D = 2048
KT = D // P
NC = 512
TICKS = KT // 2
QUARTERS = 4
RING = 4
A_W = D // 2
GROUPS = A_W // P
LAYERS = 2
DFF = 4 * D
FGROUPS = DFF // D
HG = 4
L0_HEADS = 8
L1_GROUPS = 4
SCALE = float(P) ** -0.5
RMS_EPS = 1e-6
LN_EPS = 1e-5
TRI = 3 * P
FAR = 1e30
ROW_HALVES = [(b, slice(h * D // 2, (h + 1) * D // 2)) for b in range(TB) for h in range(2)]
WARM_UP = 8
X_PARTS = 4

U_IN0, U_OUT0, U_FFN0, U_IN1, U_OUT1, U_FFN1, UNITS = 0, 10, 14, 46, 58, 62, 94
OUT_ORDER = ([(u, s) for u in range(3) for s in range(6)] + [(u, s) for u in range(3) for s in (6, 7)]
             + [(3, s) for s in range(8)])
OUT_BUF = [0, 1, 2, 0]
OUT_POST = {20: 0, 22: 1, 24: 2}


def shape_constants():
    p = np.arange(P)[:, None]
    j = np.arange(P)[None, :]
    dist = np.concatenate([p - j, p + P - j, p - j], axis=1)
    causal = dist >= 0
    count = (causal & (dist <= 128)).astype(np.float32) + (causal & (dist % 4 == 0)) + (causal & (dist % 16 == 0))
    far = np.where(count > 0, dist, FAR)
    strict = p < j
    keep = np.concatenate([strict, np.ones((P, P), bool), strict], axis=1)
    mask = np.where(keep, 0.0, -FAR)
    suffix = np.where(p >= j, -1.0, 0.0)
    return np.concatenate([np.eye(P), suffix, -np.ones((P, P)), far, count, mask], axis=1).astype(np.float32)


def trunk_kernel(nc, x_in, pre_mix, post_mix, pre_ffn, post_ffn, ab_w_in, ln_g, ln_b, sgu_w, sgu_b,
                 ab_w_out, sb_w_in, sb_w_out, ffn_w1, ffn_w2, shapes, out):
    ctx = ExitStack()
    with ctx:
        def sb(name, shape, dt=F32):
            return ctx.enter_context(nc.sbuf_tensor(name, shape, dt))

        def sem(name):
            return ctx.enter_context(nc.semaphore(name))

        x_sb = sb("x_sb", [P, TB, D])
        y_sb = sb("y_sb", [P, TB, D])
        act_hi = sb("act_hi", [P, KT, T], F32R)
        act_lo = sb("act_lo", [P, KT, T], F32R)
        hid_hi = sb("hid_hi", [P, KT, T], F32R)
        hid_lo = sb("hid_lo", [P, KT, T], F32R)
        w_raw = sb("w_raw", [P, QUARTERS, 4, NC])
        w_hi = sb("w_hi", [P, RING, 2, NC], F32R)
        w_lo = sb("w_lo", [P, RING, 2, NC], F32R)
        gpost = sb("gpost", [P, D])
        cst = sb("cst", [P, 3 * TRI + 3 * P])
        gpre = sb("gpre", [P, 4 * KT])
        qT = sb("qT", [P, HG, T])
        kT = sb("kT", [P, HG, T])
        v_sb = sb("v_sb", [P, TB, NC])
        soft_hi = sb("soft_hi", [P, 2, TRI], F32R)
        soft_lo = sb("soft_lo", [P, 2, TRI], F32R)
        sum_mats = sb("sum_mats", [P, 2 * P], F32R)
        zs = sb("zs", [P, HG, TRI])
        tmp = sb("tmp", [P, HG, TRI])
        ssy = sb("ssy", [P, TB, 4])
        ssx = sb("ssx", [P, TB, 2])
        rst = sb("rst", [P, 10])
        neg_half = sb("neg_half", [P, 2])
        warm = sb("warm", [P, 2])
        rs_bc = sb("rs_bc", [P, T])
        bn = sb("bn", [P, TB, 2, 6])
        bna = sb("bna", [P, TB, 2])
        mx = sb("mx", [P, 2, HG])
        den = sb("den", [P, 2, HG])
        rden = sb("rden", [P, 2, HG])
        ps = ctx.enter_context(nc.psum_tensor("ps", [P, 8, 512], F32))

        ident, minus_ones = cst[:, 0:P], cst[:, 2 * P:3 * P]
        far_c, count_c, mask_c = (cst[:, 3 * P + i * TRI:3 * P + (i + 1) * TRI] for i in range(3))
        va_n = y_sb[:, 0, :].rearrange("p (b c) -> p b c", b=TB)
        uT = y_sb[:, 1, :].rearrange("p (f t) -> p f t", t=T)
        sgu_nat = v_sb[:, :, :].rearrange("p b (g j) -> p (b g) j", j=P)
        sgu_bb = v_sb[:, :, :].rearrange("p b (g j) -> p (b g) j", j=P)
        sgu_wT = zs[:, :, :].rearrange("p h c -> p (h c)")[:, 0:GROUPS * P].rearrange("p (g i) -> p g i", i=P)
        gain_rows = tmp[0:4 * KT, HG - 1, 0:P]
        relu_t, sq_t = qT, kT
        junk = tmp[:, 0:HG, :].rearrange("p h c -> p (h c)")
        junk_x = zs[:, 0:HG, :].rearrange("p h c -> p (h c)")
        rs_rep = junk[:, 0:T].rearrange("p (b j) -> p b j", b=TB)
        rs_tiles = rs_bc[:, :].unsqueeze(1).broadcast_to([P, HG, T])
        gated = [junk[:, i * 512:(i + 1) * 512].rearrange("p (g t) -> p g t", t=T) for i in (1, 2)]
        lng_b, lnb_b = gpost[:, 0:A_W], gpost[:, A_W:D]

        def bank2(b):
            return ps[:, 2 * b:2 * b + 2, :]

        def bank2_tiles(b):
            return bank2(b).rearrange("p b (f t) -> p (b f) t", t=T)

        s_x = [sem(f"s_x{i}") for i in range(3)]
        s_id = sem("s_id")
        s_cst = sem("s_cst")
        s_ones = sem("s_ones")
        s_row0 = sem("s_row0")
        s_rows = sem("s_rows")
        s_sguw = sem("s_sguw")
        s_sgub = sem("s_sgub")
        s_bias = sem("s_bias")
        raw_landed = [sem(f"raw_landed{i}") for i in range(QUARTERS)]
        s_w0 = sem("s_w0")
        s_gp = sem("s_gp")
        s_out = sem("s_out")
        hi_ready = sem("hi_ready")
        lo_ready = sem("lo_ready")
        pe_ticks = sem("pe_ticks")
        s_block0 = sem("s_block0")
        post_done = sem("post_done")
        act_post = sem("act_post")
        s_tril = sem("s_tril")
        s_half = sem("s_half")
        s_warm = sem("s_warm")
        s_mean = sem("s_mean")
        s_pow = sem("s_pow")
        s_prepT = sem("s_prepT")
        s_prep = sem("s_prep")
        s_ssx = sem("s_ssx")
        s_ssy = sem("s_ssy")
        s_yg = sem("s_yg")
        s_ysum = sem("s_ysum")
        s_yl = sem("s_yl")
        s_xupd = sem("s_xupd")
        s_dve = sem("s_dve")
        s_rep = sem("s_rep")
        s_rt = sem("s_rt")
        s_tr = sem("s_tr")
        s_ehi = sem("s_ehi")
        s_elo = sem("s_elo")
        s_y0 = sem("s_y0")
        f_relu, f_sq, f_hi = sem("f_relu"), sem("f_sq"), sem("f_hi")
        s_ln = sem("s_ln")
        s_mix, s_sgt, s_gate, s_ghi, s_glo = (sem(n) for n in ("s_mix", "s_sgt", "s_gate", "s_ghi", "s_glo"))
        s_sc = sem("s_sc")
        s_zs = sem("s_zs")
        s_sm = sem("s_sm")
        s_ex = sem("s_ex")
        s_pn = sem("s_pn")
        s_pT = sem("s_pT")
        s_pc = sem("s_pc")
        s_ab = sem("s_ab")
        s_sp = sem("s_sp")
        s_sums = sem("s_sums")
        s_sphi = sem("s_sphi")
        s_splo = sem("s_splo")
        s_S = sem("s_S")
        s_e = sem("s_e")
        s_a = sem("s_a")
        s_o = sem("s_o")
        s_ohi = sem("s_ohi")
        s_olo = sem("s_olo")

        block = ctx.enter_context(nc.Block())

        @block.sync
        def _(sp):
            def load_quarter(u, q, w, k0, col):
                if not (isinstance(u, int) and u == 0):
                    sp.wait_ge(lo_ready, 8 * u + (2 * q - 6))
                src = w[bass.ds(k0 + 4 * P * q, 4 * P), bass.ds(col, NC)].rearrange("(k p) n -> p k n", p=P)
                sp.dma_start(w_raw[:, q, :, :], src).then_inc(raw_landed[q], 16)

            def load_unit(u, w, k0, col):
                for q in range(QUARTERS):
                    load_quarter(u, q, w, k0, col)

            def load_out(u0, w):
                at = 0
                for u, s in OUT_ORDER:
                    if s % 2 == 0:
                        sp.wait_ge(lo_ready, 8 * u0 + 2 * at - 6)
                        src = w[4 * P * (s // 2):4 * P * (s // 2 + 1), u * NC:(u + 1) * NC]
                        sp.dma_start(w_raw[:, at % 4, :, :], src.rearrange("(k p) n -> p k n", p=P)
                                     ).then_inc(raw_landed[at % 4], 16)
                        at += 1

            def load_gain(gain, layer, free_after):
                sp.wait_ge(post_done, free_after)
                sp.dma_start(gpost[:, :], gain[layer:layer + 1, :].partition_broadcast(P)
                             ).then_inc(s_gp, 16)

            def load_ffn(u0, layer):
                w1, w2 = ffn_w1[layer], ffn_w2[layer]
                with sp.Fori(0, FGROUPS - 1) as g:
                    with sp.Fori(0, 4) as j:
                        load_unit(u0 + 8 * g + j, w1, 0, (4 * g + j) * NC)
                    with sp.Fori(0, 4) as j:
                        load_unit(u0 + 8 * g + 4 + j, w2, g * D, j * NC)
                load_gain(post_ffn, layer, u0 + 1)
                g = FGROUPS - 1
                with sp.Fori(0, 4) as j:
                    load_unit(u0 + 8 * g + j, w1, 0, (4 * g + j) * NC)
                with sp.Fori(0, 4) as j:
                    load_unit(u0 + 8 * g + 4 + j, w2, g * D, j * NC)

            def load_x(i, cols):
                sp.dma_start(x_sb[:, :, cols], x_in[0][:, cols].rearrange("(b p) d -> p b d", p=P)
                             ).then_inc(s_x[i], 16)

            def load_first(i, signal):
                src = ab_w_in[0][2 * P * i:2 * P * (i + 1), 2 * NC:3 * NC]
                sp.dma_start(w_raw[:, 0, 2 * i:2 * i + 2, :], src.rearrange("(k p) n -> p k n", p=P)
                             ).then_inc(signal, 16)

            load_x(0, slice(0, D // 4))
            load_first(0, s_w0)
            load_first(1, raw_landed[0])
            load_x(1, slice(D // 4, D // 2))
            load_quarter(0, 1, ab_w_in[0], 0, 2 * NC)
            load_x(2, slice(D // 2, D))
            for q in (2, 3):
                load_quarter(0, q, ab_w_in[0], 0, 2 * NC)
            sp.dma_start(sgu_nat, sgu_w[0].rearrange("g i j -> i g j")).then_inc(s_sguw, 16)
            sp.dma_start(lng_b, ln_g[0:1, :].partition_broadcast(P)).then_inc(s_sgub, 16)
            sp.dma_start(lnb_b, ln_b[0:1, :].partition_broadcast(P)).then_inc(s_sgub, 16)
            load_unit(1, ab_w_in[0], 0, 3 * NC)
            sp.dma_start(cst[:, 3 * P:], shapes[:, 3 * P:]).then_inc(s_cst, 16)
            for u, c in ((2, 0), (3, 1)):
                load_unit(u, ab_w_in[0], 0, c * NC)
            sp.wait_ge(s_prepT, 4)
            sp.dma_start(v_sb[:, :, :].rearrange("p b n -> p (b n)"),
                         sgu_b[0:1].rearrange("o g i -> o (g i)").partition_broadcast(P)).then_inc(s_bias, 16)
            with sp.Fori(0, 2) as g:
                for i in range(3):
                    load_unit(4 + 3 * g + i, ab_w_in[0], 0, (4 + 2 * i + g) * NC)
            load_gain(post_mix, 0, 5)
            load_out(U_OUT0, ab_w_out[0])
            load_ffn(U_FFN0, 0)
            with sp.Fori(0, L1_GROUPS) as g:
                for i in range(3):
                    load_unit(U_IN1 + 3 * g + i, sb_w_in[0], 0, (4 * i + g) * NC)
            load_gain(post_mix, 1, U_IN1)
            load_out(U_OUT1, sb_w_out[0])
            load_ffn(U_FFN1, 1)
            for b, first, end in ((0, 0, 2), (0, 2, 4), (1, 0, 2), (1, 2, 3), (1, 3, 4)):
                sp.wait_ge(s_xupd, 2 * X_PARTS * 3 + X_PARTS * b + end)
                cols = slice(first * D // X_PARTS, end * D // X_PARTS)
                sp.dma_start(out[0, b * P:(b + 1) * P, cols], x_sb[:, b, cols]).then_inc(s_out, 16)
            sp.wait_ge(s_out, 16 * 5)

        @block.gpsimd
        def _(pool):
            nc.gpsimd.memset(rs_bc[:, :], 0.0).then_inc(s_warm, 1)
            nc.gpsimd.memset(neg_half[:, :], -0.5).then_inc(s_half, 1)
            pool.wait_ge(s_half, 1)
            done = 0

            def power(cols):
                nonlocal done
                done += 1
                pool.wait_ge(s_mean, done)
                nc.gpsimd.tensor_tensor(rst[:, cols], rst[:, cols], neg_half[:, 0:cols.stop - cols.start], ALU.pow
                                        ).then_inc(s_pow, 1)

            rs_y0, rs_y1, rs_x, rs_ln = slice(2, 3), slice(3, 4), slice(6, 8), slice(8, 10)
            power(rs_x)
            pool.wait_ge(s_sguw, 16)
            nc.gpsimd.affine_select(out=sgu_nat, in_=sgu_nat, compare_op=ALU.is_ge, fill=0.0, base=0,
                                    pattern=[[0, GROUPS], [-1, P]], channel_multiplier=1).then_inc(s_tril, 1)
            power(rs_ln)
            for layer in range(LAYERS):
                for cols in (rs_y0, rs_y1, rs_x):
                    power(cols)
                pool.wait_ge(s_xupd, 2 * X_PARTS * (2 * layer + 1))
                nc.gpsimd.memset(y_sb[:, :, :], 0.0).then_inc(s_y0, 1)
                for cols in (rs_y0, rs_y1, rs_x) if layer == 0 else (rs_y0, rs_y1):
                    power(cols)

        @block.scalar
        def _(act):
            def conv(u, t):
                if isinstance(u, int) and 8 * u + t == 0:
                    act.wait_ge(s_w0, 16)
                else:
                    act.wait_ge(raw_landed[t // 2], 16 * (u + 1))
                if not (isinstance(u, int) and 8 * u + t < RING):
                    act.wait_ge(pe_ticks, 8 * u + (t - RING + 1))
                h = 2 * (t % 2)
                nc.scalar.activation(w_hi[:, t % RING, :, :], w_raw[:, t // 2, h:h + 2, :], ACT.Copy
                                     ).then_inc(hi_ready, 1)

            def conv_at(u, t):
                if t < 4:
                    conv(u, t + 4)
                elif not (isinstance(u, int) and u == UNITS - 1):
                    conv(u + 1, t - 4)

            def unit(u, post, extras=None, first=1):
                for t in range(first, TICKS):
                    for f in (extras or {}).get(t, []):
                        f()
                    conv_at(u, t)
                post()
                if not (isinstance(u, int) and u == UNITS - 1):
                    conv(u + 1, 4)

            def unit_finished(u):
                act.wait_ge(pe_ticks, 8 * u + 8)

            def nothing():
                pass

            def evacuate(k, j):
                act.wait_ge(s_tr, 8 * k + j + 1)
                b = 2 + j if j < 6 else j - 4
                for i in range(2):
                    kt = 2 * j + i
                    last = nc.scalar.activation(act_hi[:, kt, :], ps[:, b, i * T:(i + 1) * T], ACT.Copy,
                                                scale=gpre[:, k * KT + kt:k * KT + kt + 1])
                last.then_inc(s_ehi, 1)

            def fill(k, u):
                for j in range(8):
                    if 2 <= j < 5 or k == 0 and j > 0:
                        conv(u, j)
                    evacuate(k, j)
                    if k == 0 and j >= 4:
                        squares_x_half(k, j - 4)
                    elif k and j in (3, 4):
                        squares_x_half(k, j - 1)

            squares = [0, 0]

            def junk_free():
                for semaphore, n in zip((s_ssx, s_ssy), squares):
                    if n:
                        act.wait_ge(semaphore, n)

            def squares_x_half(k, i):
                b, half = ROW_HALVES[i]
                if k:
                    act.wait_ge(s_xupd, 2 * X_PARTS * (k - 1) + 2 * (i + 1))
                else:
                    for semaphore in ((s_x[2],) if i % 2 else s_x[0:2]):
                        act.wait_ge(semaphore, 16)
                junk_free()
                squares[0] += 1
                nc.scalar.activation(junk_x[:, 0:D // 2], x_sb[:, b, half], ACT.Square,
                                     accum_out=ssx[:, b, i % 2:i % 2 + 1]).then_inc(s_ssx, 1)

            def square_y(src, c, b):
                junk_free()
                squares[1] += 1
                nc.scalar.activation(junk[:, 2 * NC:3 * NC], src, ACT.Square, accum_out=ssy[:, b, c:c + 1]
                                     ).then_inc(s_ssy, 1)

            def transition(k, u, source, ready):
                for b in range(TB):
                    ready(b)
                    square_y(source[b], 3, b)
                    if k < 4:
                        if b == 0:
                            conv(u, 0)
                            conv(u, 1)
                        else:
                            squares_x_half(k, 0)
                            squares_x_half(k, 1)
                            fill(k, u)

            def l0_exp(grp):
                act.wait_ge(s_sm, 4 * grp + 4)
                nc.scalar.activation(zs[:, :, :], zs[:, :, :], ACT.Exp).then_inc(s_ex, 1)

            def l0_copy_pT(n):
                act.wait_ge(s_pT, n + 1)
                b = 2 * (n % 2)
                nc.scalar.activation(tmp[:, b:b + 2, :], ps[:, 6:8, 0:TRI], ACT.Copy).then_inc(s_pc, 1)

            def o_hi(n, b, tile):
                act.wait_ge(s_o, n + 1)
                nc.scalar.activation(hid_hi[:, bass.ds(tile, 2), :],
                                     ps[:, 6 + b, :].rearrange("p (h t) -> p h t", t=T), ACT.Copy).then_inc(s_ohi, 1)

            def l0_extras(grp):
                return {9: [lambda: l0_exp(grp)], 13: [lambda: l0_copy_pT(2 * grp)],
                        14: [lambda: l0_copy_pT(2 * grp + 1)],
                        15: [lambda: o_hi(2 * grp, 0, 8 + 4 * grp)],
                        17: [lambda: o_hi(2 * grp + 1, 1, 8 + 4 * grp + 2)]}

            def l1_logs(b, grp):
                pair = 2 * grp + b
                z, t = zs[:, 2 * b:2 * b + 2, :], tmp[:, 0:2, :]
                act.wait_ge(s_zs, 4 * grp + (L0_HEADS + 2 * b + 2))
                if b == 1:
                    act.wait_ge(s_sp, pair)
                nc.scalar.activation(t, z, ACT.Abs).then_inc(s_ab, 1)
                act.wait_ge(s_ab, 3 * pair + 1)
                nc.scalar.activation(t, t, ACT.Exp, scale=-1.0).then_inc(s_ab, 1)
                act.wait_ge(s_ab, 3 * pair + 2)
                nc.scalar.activation(t, t, ACT.Ln, bias=1.0).then_inc(s_ab, 1)

            def l1_soft_hi(b, grp):
                act.wait_ge(s_sp, 2 * grp + (b + 1))
                nc.scalar.activation(soft_hi[:, :, :], tmp[:, 2:4, :], ACT.Copy).then_inc(s_sphi, 1)

            def l1_weights(b, grp):
                z = zs[:, 2 * b:2 * b + 2, :]
                act.wait_ge(s_e, 2 * grp + (b + 1))
                nc.scalar.activation(z, z, ACT.Exp).then_inc(s_a, 1)

            def l1_extras(grp):
                return {4: [lambda: l1_logs(0, grp)], 6: [lambda: l1_soft_hi(0, grp), lambda: l1_logs(1, grp)],
                        10: [lambda: l1_weights(0, grp), lambda: l1_soft_hi(1, grp)],
                        12: [lambda: o_hi(2 * grp + 4, 0, 4 * grp)],
                        15: [lambda: l1_weights(1, grp)], 17: [lambda: o_hi(2 * grp + 5, 1, 4 * grp + 2)]}

            def qkv_group(u, extras):
                for i in range(3):
                    unit(u + i, nothing, {t - 8 * i: f for t, f in extras.items() if 8 * i < t < 8 * i + 8})

            def sum_squares_psum(u0, c):
                for b in range(TB):
                    if b:
                        act.wait_ge(s_yg, 6 * (u0 == U_OUT1) + 2 * c + 1)
                    square_y(ps[:, 2 * OUT_BUF[c] + b, :], c, b)

            def out_phase(u0, extras, k):
                for t in range(1, 28):
                    for f in extras.get(t, []):
                        f()
                    if t in OUT_POST:
                        act.wait_ge(pe_ticks, 8 * u0 + t)
                        sum_squares_psum(u0, OUT_POST[t])
                    conv_at(u0 + t // 8, t % 8)

                def ready(b):
                    if b == 0:
                        act.wait_ge(s_block0, k)
                    else:
                        act.wait_ge(pe_ticks, 8 * u0 + 32)
                transition(k, u0 + 4, [ps[:, b, :] for b in range(TB)], ready)

            def ffn(u0, layer):
                f0 = 16 * layer

                def up(g, jj, par):
                    u, f = u0 + 8 * g + 2 * jj + par, f0 + 4 * g + 2 * jj + par

                    def post():
                        act.wait_ge(f_relu, f + 1)
                        act.wait_ge(post_done, u)
                        nc.scalar.activation(sq_t[:, :, :], relu_t[:, :, :], ACT.Square).then_inc(f_sq, 1)
                        act.wait_ge(f_sq, f + 1)
                        nc.scalar.activation(hid_hi[:, bass.ds(8 * jj + 4 * par, 4), :], sq_t[:, :, :], ACT.Copy
                                             ).then_inc(f_hi, 1)
                    unit(u, post)

                def group_up(g):
                    with act.Fori(0, 2) as jj:
                        for par in range(2):
                            up(g, jj, par)

                with act.Fori(0, FGROUPS - 1) as g:
                    group_up(g)
                    with act.Fori(0, 2) as jj:
                        for par in range(2):
                            unit(u0 + 8 * g + 4 + 2 * jj + par, nothing)
                group_up(FGROUPS - 1)
                total = [junk[:, b * NC:(b + 1) * NC] for b in range(TB)]
                u = u0 + 8 * (FGROUPS - 1) + 4

                def ready(b, j=3):
                    act.wait_ge(s_ysum, 8 * layer + 2 * j + b + 1)

                for j in range(3):
                    def post(j=j):
                        for b in range(TB):
                            ready(b, j)
                            square_y(total[b], j, b)
                    unit(u + j, post)
                for t in range(1, 4):
                    conv_at(u + 3, t)
                transition(2 * layer + 2, u + 4, total, ready)

            def load_gain_rows(i, g, l, signal):
                act.dma_start(tmp[i * KT:(i + 1) * KT, HG - 1, 0:P], g[l].rearrange("(k p) -> k p", p=P)
                              ).then_inc(signal, 16)

            load_gain_rows(0, pre_mix, 0, s_row0)
            act.dma_start(ident, shapes[:, 0:P]).then_inc(s_id, 16)
            act.dma_start(cst[:, P:3 * P], shapes[:, P:3 * P]).then_inc(s_ones, 16)
            act.wait_ge(s_half, 1)
            nc.scalar.activation(warm[:, :], neg_half[:, :], ACT.Gelu)
            for i, (g, l) in enumerate(((pre_ffn, 0), (pre_mix, 1), (pre_ffn, 1))):
                load_gain_rows(i + 1, g, l, s_rows)
            conv(0, 0)
            act.wait_ge(s_prepT, 1)
            nc.scalar.activation(gpre[:, 0:KT], ps[:, 0, 0:KT], ACT.Copy).then_inc(s_prep, 1)
            act.wait_ge(s_prep, 1)
            fill(0, 0)

            def gelu_v(j):
                unit_finished(j)
                act.wait_ge(s_pow, 1)
                for b in range(TB):
                    last = nc.scalar.activation(va_n[:, b, j * NC:(j + 1) * NC], ps[:, 2 * j + b, :], ACT.Gelu,
                                                scale=rst[:, 6 + b:7 + b])
                last.then_inc(act_post, 1)

            def gelu_u(j):
                act.wait_ge(post_done, 3 + j)
                nc.scalar.activation(uT[:, 4 * j:4 * j + 4, :], (qT, kT)[j][:, :, :], ACT.Gelu).then_inc(act_post, 1)

            def gate_hi(m):
                act.wait_ge(s_gate, m + 1)
                nc.scalar.activation(hid_hi[:, 2 * m:2 * m + 2, :],
                                     gated[m % 2], ACT.Copy).then_inc(s_ghi, 1)

            def small_parts():
                act.wait_ge(s_prepT, 2)
                nc.scalar.activation(gpre[:, KT:4 * KT], ps[:, 5, KT:4 * KT], ACT.Copy).then_inc(s_prep, 1)
                act.wait_ge(s_prepT, 4)
                act.wait_ge(s_ssx, 4)
                nc.scalar.activation(sgu_wT, ps[:, 6:8, :].rearrange("p b (g i) -> p (b g) i", i=P), ACT.Copy
                                     ).then_inc(s_prep, 1)

            unit(0, lambda: gelu_v(0), first=4)
            unit(1, lambda: gelu_v(1), {6: [small_parts]})
            for j in range(2):
                unit(2 + j, lambda j=j: gelu_u(j))
            qkv_group(4, {m + 2: [lambda m=m: gate_hi(m)] for m in range(4)})
            qkv_group(7, l0_extras(0))
            out_phase(U_OUT0, l0_extras(1), 1)
            ffn(U_FFN0, 0)

            def suffix_matrices():
                nc.scalar.activation(sum_mats[:, :], cst[:, P:3 * P], ACT.Copy).then_inc(s_sums, 1)

            qkv_group(U_IN1, {9: [suffix_matrices]})
            with act.Fori(1, L1_GROUPS) as g:
                qkv_group(U_IN1 + 3 * g, l1_extras(g - 1))
            out_phase(U_OUT1, l1_extras(L1_GROUPS - 1), 3)
            ffn(U_FFN1, 1)

        @block.vector
        def _(dve):
            steps, powers = [0], [0]

            def chain(ins):
                steps[0] += 1
                ins.then_inc(s_dve, 1)
                dve.wait_ge(s_dve, steps[0])

            def conv(u, t):
                dve.wait_ge(hi_ready, 8 * u + (t + 1))
                h = 2 * (t % 2)
                nc.vector.tensor_tensor(w_lo[:, t % RING, :, :], w_raw[:, t // 2, h:h + 2, :],
                                        w_hi[:, t % RING, :, :].bitcast(F32), ALU.subtract).then_inc(lo_ready, 1)

            def conv_at(u, t):
                if t < 4:
                    conv(u, t + 4)
                elif not (isinstance(u, int) and u == UNITS - 1):
                    conv(u + 1, t - 4)

            def unit(u, post, extras=None, first=1):
                for t in range(first, TICKS):
                    for f in (extras or {}).get(t, []):
                        f()
                    conv_at(u, t)
                post()
                if not (isinstance(u, int) and u == UNITS - 1):
                    conv(u + 1, 4)

            def unit_finished(u):
                dve.wait_ge(pe_ticks, 8 * u + 8)

            def rsqrt(dst, src, scale, eps):
                nc.vector.tensor_scalar(dst, src, scale, eps, ALU.mult, ALU.add).then_inc(s_mean, 1)
                powers[0] += 1
                dve.wait_ge(s_pow, powers[0])

            def raise_power(ins):
                ins.then_inc(s_mean, 1)
                powers[0] += 1
                return powers[0]

            def update_x(k, b, power, parts):
                dve.wait_ge(s_pow, power)
                dve.wait_ge(s_yl, 2 * k - 1 + b)
                for i in parts:
                    cols = slice(i * D // X_PARTS, (i + 1) * D // X_PARTS)
                    nc.vector.scalar_tensor_tensor(x_sb[:, b, cols], y_sb[:, b, cols], rst[:, 2 + b:3 + b],
                                                   x_sb[:, b, cols], ALU.mult, ALU.add).then_inc(s_xupd, 1)

            def evacuate(k, j):
                dve.wait_ge(s_ehi, 8 * k + j + 1)
                b = 2 + j if j < 6 else j - 4
                for i in range(2):
                    kt = 2 * j + i
                    last = nc.vector.scalar_tensor_tensor(
                        act_lo[:, kt, :], ps[:, b, i * T:(i + 1) * T], gpre[:, k * KT + kt:k * KT + kt + 1],
                        act_hi[:, kt, :].bitcast(F32), ALU.mult, ALU.subtract)
                last.then_inc(s_elo, 1)

            def fill(k, u):
                for j in range(8):
                    if k == 0 or 1 <= j < 5:
                        conv(u, j)
                    if k == 0 or j >= 1:
                        evacuate(k, j)
                    if k and j == 5:
                        power = mean_x(k)
                    if k and j == 6:
                        scale_rows(power)
                if k:
                    scale_tiles(k)

            def mean_x(k):
                dve.wait_ge(s_ssx, 4 * (k + 1))
                chain(nc.vector.tensor_reduce(rst[:, 4:6], ssx[:, :, :], AX.X, ALU.add))
                return raise_power(nc.vector.tensor_scalar(rst[:, 6:8], rst[:, 4:6], 1.0 / D, RMS_EPS,
                                                           ALU.mult, ALU.add))

            def scale_rows(power):
                dve.wait_ge(s_pow, power)
                for b in range(TB):
                    nc.vector.tensor_scalar(rs_rep[:, b, :], minus_ones, rst[:, 6 + b:7 + b], -1.0,
                                            ALU.mult, ALU.mult).then_inc(s_rep, 1)

            def scale_tiles(k):
                dve.wait_ge(s_rt, k + 1)
                chain(nc.vector.tensor_copy(rs_bc[:, :], ps[:, 4, 0:T]))

            def transition(k, u, take):
                dve.wait_ge(s_ssy, 8 * (k - 1) + 6)
                chain(nc.vector.tensor_reduce(rst[:, 0:2], ssy[:, :, 0:3], AX.X, ALU.add))
                chain(nc.vector.tensor_scalar(rst[:, 0:2], rst[:, 0:2], 1.0 / D, RMS_EPS, ALU.mult, ALU.add))

                def mean_y(b):
                    dve.wait_ge(s_ssy, 8 * (k - 1) + 7 + b)
                    return raise_power(nc.vector.tensor_scalar(rst[:, 2 + b:3 + b], ssy[:, b, 3:4], 1.0 / D,
                                                               rst[:, b:b + 1], ALU.mult, ALU.add))

                take(0, 0)
                power = mean_y(0)
                take(0, 1)
                update_x(k, 0, power, range(X_PARTS))
                if k in (1, 3):
                    conv(u, 0)
                take(1, 0)
                power = mean_y(1)
                take(1, 1)
                dve.sem_inc(post_done, 1)
                if k == 4:
                    update_x(k, 1, power, range(X_PARTS))
                    return
                update_x(k, 1, power, range(2))
                if k == 2:
                    conv(u, 0)
                evacuate(k, 0)
                update_x(k, 1, power, range(2, X_PARTS))
                fill(k, u)

            def l0_scores(h, head):
                dve.wait_ge(s_sc, head + 1)
                dve.wait_ge(s_cst, 16)
                nc.vector.scalar_tensor_tensor(zs[:, h, :], far_c, -(2.0 ** -(head + 1)), ps[:, 6 + h % 2, 0:TRI],
                                               ALU.mult, ALU.add).then_inc(s_zs, 1)

            def halves(t):
                return t[:, :, 0:P], t[:, :, P:TRI]

            def l0_max(grp):
                dve.wait_ge(s_zs, 4 * grp + 4)
                for i, z in enumerate(halves(zs)):
                    nc.vector.tensor_reduce(mx[:, i, :], z, AX.X, ALU.max).then_inc(s_sm, 1)

            def l0_less_max(grp):
                dve.wait_ge(s_sm, 4 * grp + 2)
                for i, z in enumerate(halves(zs)):
                    m = mx[:, i, :].unsqueeze(2).broadcast_to([P, HG, z.shape[2]])
                    nc.vector.tensor_tensor(z, z, m, ALU.subtract).then_inc(s_sm, 1)

            def l0_count(grp):
                dve.wait_ge(s_ex, grp + 1)
                chain(nc.vector.tensor_tensor(zs[:, :, :], zs[:, :, :],
                                              count_c.unsqueeze(1).broadcast_to([P, HG, TRI]), ALU.mult))

            def l0_normalise(grp):
                for i, z in enumerate(halves(zs)):
                    chain(nc.vector.tensor_reduce(den[:, i, :], z, AX.X, ALU.add))
                chain(nc.vector.reciprocal(rden[:, :, :], den[:, :, :]))
                for i, z in enumerate(halves(zs)):
                    m = rden[:, i, :].unsqueeze(2).broadcast_to([P, HG, z.shape[2]])
                    nc.vector.tensor_tensor(z, z, m, ALU.mult).then_inc(s_pn, 1)

            def o_lo(n, b, tile):
                dve.wait_ge(s_ohi, n + 1)
                nc.vector.tensor_tensor(hid_lo[:, bass.ds(tile, 2), :], ps[:, 6 + b, :].rearrange("p (h t) -> p h t", t=T),
                                        hid_hi[:, bass.ds(tile, 2), :].bitcast(F32), ALU.subtract).then_inc(s_olo, 1)

            def l0_extras(grp):
                e = {2 + h: [lambda h=h: l0_scores(h, 4 * grp + h)] for h in range(4)}
                e.update({6: [lambda: l0_max(grp)], 7: [lambda: l0_less_max(grp)], 9: [lambda: l0_count(grp)],
                          10: [lambda: l0_normalise(grp)], 15: [lambda: o_lo(2 * grp, 0, 8 + 4 * grp)],
                          17: [lambda: o_lo(2 * grp + 1, 1, 8 + 4 * grp + 2)]})
                return e

            def l1_scores(h, grp):
                dve.wait_ge(s_sc, 4 * grp + (L0_HEADS + h + 1))
                nc.vector.tensor_tensor(zs[:, h, :], ps[:, 6 + h % 2, 0:TRI], mask_c, ALU.add).then_inc(s_zs, 1)

            def l1_softplus(b, grp):
                dve.wait_ge(s_ab, 6 * grp + 3 * b + 3)
                nc.vector.scalar_tensor_tensor(tmp[:, 2:4, :], zs[:, 2 * b:2 * b + 2, :], 0.0, tmp[:, 0:2, :],
                                               ALU.max, ALU.add).then_inc(s_sp, 1)

            def l1_exponent(b, grp):
                dve.wait_ge(s_S, 2 * grp + (b + 1))
                for z, sums in ((zs[:, 2 * b:2 * b + 2, 0:T], ps[:, 6, :]), (zs[:, 2 * b:2 * b + 2, T:TRI], ps[:, 7, 0:T])):
                    last = nc.vector.tensor_tensor(z, z, sums.rearrange("p (h t) -> p h t", h=2), ALU.add)
                last.then_inc(s_e, 1)

            def l1_soft_lo(b, grp):
                dve.wait_ge(s_sphi, 2 * grp + (b + 1))
                nc.vector.tensor_tensor(soft_lo[:, :, :], tmp[:, 2:4, :], soft_hi[:, :, :].bitcast(F32), ALU.subtract
                                        ).then_inc(s_splo, 1)

            def l1_extras(grp):
                e = {2 + h: [lambda h=h: l1_scores(h, grp)] for h in range(4)}
                e[5].append(lambda: l1_softplus(0, grp))
                e.update({6: [lambda: l1_soft_lo(0, grp)],
                          9: [lambda: l1_exponent(0, grp), lambda: l1_softplus(1, grp)],
                          11: [lambda: l1_soft_lo(1, grp)], 12: [lambda: o_lo(2 * grp + 4, 0, 4 * grp)],
                          14: [lambda: l1_exponent(1, grp)], 17: [lambda: o_lo(2 * grp + 5, 1, 4 * grp + 2)]})
                return e

            def qkv_group(u, extras):
                def post_q():
                    unit_finished(u)
                    nc.vector.scalar_tensor_tensor(qT[:, :, :], bank2_tiles(0), SCALE, rs_tiles, ALU.mult, ALU.mult
                                                   ).then_inc(post_done, 1)

                def post_k():
                    unit_finished(u + 1)
                    nc.vector.tensor_tensor(kT[:, :, :], bank2_tiles(1), rs_tiles, ALU.mult).then_inc(post_done, 1)

                def post_v():
                    unit_finished(u + 2)
                    for b in range(TB):
                        last = nc.vector.tensor_scalar(v_sb[:, b, :], ps[:, 4 + b, :], rst[:, 6 + b:7 + b], None, ALU.mult)
                    last.then_inc(post_done, 1)

                for i, post in enumerate((post_q, post_k, post_v)):
                    unit(u + i, post, {t - 8 * i: f for t, f in extras.items() if 8 * i < t < 8 * i + 8})

            def out_phase(u0, extras, k):
                def post(c, t):
                    dve.wait_ge(pe_ticks, 8 * u0 + t)
                    dve.wait_ge(s_gp, 16 * k)
                    cols = slice(c * NC, (c + 1) * NC)
                    for b in (1, 0):
                        if b == 0:
                            dve.wait_ge(s_ssy, 8 * (k - 1) + 2 * c + 1)
                        ins = nc.vector.tensor_tensor(y_sb[:, b, cols], ps[:, 2 * OUT_BUF[c] + b, :], gpost[:, cols],
                                                      ALU.mult)
                        ins.then_inc(s_yg, 1)
                    dve.wait_ge(s_ssy, 8 * (k - 1) + 2 * c + 2)
                    dve.wait_ge(s_yg, 6 * (k // 2) + 2 * c + 2)
                    dve.sem_inc(post_done, 1)

                for t in range(1, 28):
                    for f in extras.get(t, []):
                        f()
                    if t in OUT_POST:
                        post(OUT_POST[t], t)
                    conv_at(u0 + t // 8, t % 8)

                def take(b, step):
                    if step:
                        cols = slice(3 * NC, 4 * NC)
                        nc.vector.tensor_tensor(y_sb[:, b, cols], ps[:, b, :], gpost[:, cols], ALU.mult
                                                ).then_inc(s_yl, 1)
                        dve.wait_ge(s_yl, 2 * k - 1 + b)
                transition(k, u0 + 4, take)

            def ffn(u0, layer):
                f0 = 16 * layer

                def up(g, jj, par):
                    u, f = u0 + 8 * g + 2 * jj + par, f0 + 4 * g + 2 * jj + par

                    def post():
                        unit_finished(u)
                        nc.vector.scalar_tensor_tensor(relu_t[:, :, :], bank2_tiles(par), 0.0, rs_tiles,
                                                       ALU.max, ALU.mult).then_inc(f_relu, 1)
                        dve.wait_ge(f_hi, f + 1)
                        tiles = bass.ds(8 * jj + 4 * par, 4)
                        nc.vector.tensor_tensor(hid_lo[:, tiles, :], sq_t[:, :, :], hid_hi[:, tiles, :].bitcast(F32),
                                                ALU.subtract).then_inc(post_done, 1)
                    unit(u, post)

                def group_up(g):
                    with dve.Fori(0, 2) as jj:
                        for par in range(2):
                            up(g, jj, par)

                def add_y(u, chunk, par):
                    unit_finished(u)
                    dve.wait_ge(post_done, u)
                    ys = y_sb[:, :, bass.ds(chunk, NC)]
                    return nc.vector.tensor_tensor(ys, ys, bank2(par), ALU.add)

                with dve.Fori(0, FGROUPS - 1) as g:
                    group_up(g)
                    dve.wait_ge(s_y0, layer + 1)
                    with dve.Fori(0, 2) as jj:
                        for par in range(2):
                            u = u0 + 8 * g + 4 + 2 * jj + par
                            unit(u, lambda: add_y(u, 2 * NC * jj + NC * par, par).then_inc(post_done, 1))
                group_up(FGROUPS - 1)
                u3 = u0 + 8 * (FGROUPS - 1) + 4
                k = 2 * layer + 2
                total = [junk[:, b * NC:(b + 1) * NC] for b in range(TB)]

                def complete(j, b):
                    if j:
                        dve.wait_ge(s_ssy, 8 * (k - 1) + 2 * (j - 1) + b + 1)
                    nc.vector.tensor_tensor(total[b], y_sb[:, b, j * NC:(j + 1) * NC], ps[:, 2 * (j % 2) + b, :],
                                            ALU.add).then_inc(s_ysum, 1)
                    dve.wait_ge(s_ysum, 8 * layer + 2 * j + b + 1)

                def gained(j, b):
                    dve.wait_ge(s_gp, 16 * k)
                    cols = slice(j * NC, (j + 1) * NC)
                    return nc.vector.tensor_tensor(y_sb[:, b, cols], total[b], gpost[:, cols], ALU.mult)

                for j in range(3):
                    def post(j=j):
                        unit_finished(u3 + j)
                        dve.wait_ge(post_done, u3 + j)
                        for b in range(TB):
                            complete(j, b)
                        gained(j, 0)
                        gained(j, 1).then_inc(post_done, 1)
                    unit(u3 + j, post)
                for t in range(1, 4):
                    conv_at(u3 + 3, t)

                def take(b, step):
                    if step == 0:
                        if b == 0:
                            dve.wait_ge(s_block0, k)
                            dve.wait_ge(post_done, u3 + 3)
                        else:
                            unit_finished(u3 + 3)
                        complete(3, b)
                    else:
                        gained(3, b).then_inc(s_yl, 1)
                        dve.wait_ge(s_yl, 2 * k - 1 + b)
                transition(k, u3 + 4, take)

            dve.wait_ge(s_ones, 16)
            fill(0, 0)

            def stats_v(j):
                dve.wait_ge(act_post, j + 1)
                for b in range(TB):
                    last = nc.vector.bn_stats(bn[:, b, j, :], va_n[:, b, j * NC:(j + 1) * NC])
                last.then_inc(post_done, 1)

            def layernorm_v(step):
                if step == 0:
                    dve.wait_ge(post_done, 2)
                    for b in range(TB):
                        chain(nc.vector.bn_aggr(bna[:, b, :], bn[:, b, :, :]))
                    rsqrt(rst[:, 8:10], bna[:, :, 1], 1.0, LN_EPS)
                    for b in range(TB):
                        nc.vector.tensor_scalar(va_n[:, b, :], va_n[:, b, :], bna[:, b, 0:1], rst[:, 8 + b:9 + b],
                                                ALU.subtract, ALU.mult).then_inc(s_ln, 1)
                else:
                    dve.wait_ge(s_ln, step + 1)
                    dve.wait_ge(s_sgub, 32)
                    g = (lng_b if step == 1 else lnb_b).unsqueeze(1).broadcast_to([P, TB, A_W])
                    nc.vector.tensor_tensor(va_n, va_n, g, ALU.mult if step == 1 else ALU.add).then_inc(s_ln, 1)

            def post_u(j):
                unit_finished(2 + j)
                nc.vector.tensor_tensor((qT, kT)[j][:, :, :], bank2_tiles(j), rs_tiles, ALU.mult).then_inc(post_done, 1)

            mixed = junk[:, 0:512].rearrange("p (g c i) -> p g c i", g=2, i=P)

            def gate(m):
                dve.wait_ge(s_mix, m + 1)
                dve.wait_ge(act_post, 4)
                dve.wait_ge(s_bias, 16)
                if m:
                    dve.wait_ge(s_gate, m)
                bias = sgu_bb[:, 2 * m:2 * m + 2, :].unsqueeze(2).broadcast_to([P, 2, TB, P])
                nc.vector.tensor_tensor(mixed, ps[:, 6 + m % 2, :].rearrange("p (g c i) -> p g c i", g=2, i=P), bias,
                                        ALU.add).then_inc(s_sgt, 1)
                dve.wait_ge(s_sgt, m + 1)
                nc.vector.tensor_tensor(gated[m % 2], junk[:, 0:512].rearrange("p (g t) -> p g t", t=T),
                                        uT[:, 2 * m:2 * m + 2, :], ALU.mult).then_inc(s_gate, 1)

            def gate_lo(m):
                dve.wait_ge(s_ghi, m + 1)
                nc.vector.tensor_tensor(hid_lo[:, 2 * m:2 * m + 2, :], gated[m % 2],
                                        hid_hi[:, 2 * m:2 * m + 2, :].bitcast(F32), ALU.subtract).then_inc(s_glo, 1)

            power_x = mean_x(0)
            unit(0, lambda: stats_v(0), first=4)
            unit(1, lambda: stats_v(1), {1: [lambda: scale_rows(power_x)], 3: [lambda: scale_tiles(0)]})
            unit(2, lambda: post_u(0), {1 + i: [lambda i=i: layernorm_v(i)] for i in range(3)})
            unit(3, lambda: post_u(1))
            gates = {1: [lambda: gate(0)], 5: [lambda: gate_lo(3)]}
            for m in range(1, 4):
                gates[1 + m] = [lambda m=m: gate(m), lambda m=m: gate_lo(m - 1)]
            qkv_group(4, gates)
            qkv_group(7, l0_extras(0))
            out_phase(U_OUT0, l0_extras(1), 1)
            ffn(U_FFN0, 0)

            qkv_group(U_IN1, {})
            with dve.Fori(1, L1_GROUPS) as g:
                qkv_group(U_IN1 + 3 * g, l1_extras(g - 1))
            out_phase(U_OUT1, l1_extras(L1_GROUPS - 1), 3)
            ffn(U_FFN1, 1)

        @block.tensor
        def _(pe):
            def mm(dst, lhsT, rhs, start, stop):
                return nc.tensor.matmul(dst, lhsT, rhs, start=start, stop=stop, skip_group_check=True)

            def tick_tokens(buf, s, slot, hi, lo, ready):
                pe.wait_ge(lo_ready, ready)
                for i in range(2):
                    kt = 2 * s + i
                    for b in range(TB):
                        dst, tok = ps[:, 2 * buf + b, :], slice(b * P, (b + 1) * P)
                        mm(dst, hi[:, kt, tok], w_hi[:, slot, i, :], kt == 0, False)
                        mm(dst, hi[:, kt, tok], w_lo[:, slot, i, :], False, False)
                        last = mm(dst, lo[:, kt, tok], w_hi[:, slot, i, :], False, kt == KT - 1)
                last.then_inc(pe_ticks, 1)

            def tick_features(buf, s, slot, hi, lo, ready):
                pe.wait_ge(lo_ready, ready)
                for i in range(2):
                    kt = 2 * s + i
                    for f in range(4):
                        dst, cols = ps[:, 2 * buf + f // 2, (f % 2) * T:(f % 2 + 1) * T], slice(f * P, (f + 1) * P)
                        mm(dst, w_hi[:, slot, i, cols], hi[:, kt, :], kt == 0 and f % 2 == 0, False)
                        mm(dst, w_hi[:, slot, i, cols], lo[:, kt, :], False, False)
                        last = mm(dst, w_lo[:, slot, i, cols], hi[:, kt, :], False, kt == KT - 1)
                last.then_inc(pe_ticks, 1)

            def closing_ticks(buf, u):
                for b in range(TB):
                    for s in range(4, TICKS):
                        if b == 0:
                            pe.wait_ge(lo_ready, 8 * u + s + 1)
                        for i in range(2):
                            kt = 2 * s + i
                            dst, tok, slot = ps[:, 2 * buf + b, :], slice(b * P, (b + 1) * P), s % RING
                            mm(dst, hid_hi[:, kt, tok], w_hi[:, slot, i, :], False, False)
                            mm(dst, hid_hi[:, kt, tok], w_lo[:, slot, i, :], False, False)
                            last = mm(dst, hid_lo[:, kt, tok], w_hi[:, slot, i, :], False, kt == KT - 1)
                        if b == 1:
                            last.then_inc(pe_ticks, 1)
                    if b == 0:
                        last.then_inc(s_block0, 1)

            def unit(u, tick, buf, hi=act_hi, lo=act_lo, fresh=None, extras=None, before=None, closing=False):
                need = u if fresh is not None else u - 1
                if not (isinstance(need, int) and need <= 0):
                    pe.wait_ge(post_done, need)
                for s in range(TICKS):
                    for f in (extras or {}).get(s, []):
                        f()
                    if fresh is not None:
                        late_transposes(fresh, s)
                        pe.wait_ge(s_elo, 8 * fresh + s + 1)
                    if closing and s == 4:
                        closing_ticks(buf, u)
                        break
                    if before is not None:
                        before(s)
                    tick(buf, s, s % RING, hi, lo, 8 * u + (s + 1))

            def transpose_pair(j, b):
                bank = 2 + j if j < 6 else j - 4
                for i in range(2):
                    kt = 2 * j + i
                    last = nc.tensor.transpose(ps[:, bank, i * T + b * P:i * T + (b + 1) * P],
                                               x_sb[:, b, kt * P:(kt + 1) * P], ident)
                return last

            def transposes(k, u):
                def updated(b, j):
                    pe.wait_ge(s_xupd, 2 * X_PARTS * (k - 1) + X_PARTS * b + j // 2 + 1)

                pe.wait_ge(post_done, u - 1)
                for j in (2, 3, 4, 5):
                    if j % 2 == 0:
                        updated(0, j)
                    transpose_pair(j, 0)
                pe.wait_ge(post_done, u)
                for j in (0, 1):
                    transpose_pair(j, 0)
                for j in range(4):
                    if j % 2 == 0:
                        updated(1, j)
                    transpose_pair(j, 1).then_inc(s_tr, 1)

            def late_transposes(k, s):
                if k == 0:
                    pairs = (0, 1) if s == 0 else (s + 1,) if s < 7 else ()
                    if s in (0, 1, 3):
                        pe.wait_ge(s_x[(s + 1) // 2], 16)
                else:
                    pairs = {1: (4, 5, 6), 2: (7,)}.get(s, ())
                    if s == 1:
                        pe.wait_ge(s_xupd, 2 * X_PARTS * k)
                for j in pairs:
                    if j >= 6:
                        pe.wait_ge(s_elo, 8 * k + j - 5)
                    if k == 0 or j >= 6:
                        transpose_pair(j, 0)
                    transpose_pair(j, 1).then_inc(s_tr, 1)
                if k and s == 4:
                    transpose_scales(k)

            def transpose_scales(k):
                pe.wait_ge(s_rep, 2 * (k + 1))
                for b in range(TB):
                    last = nc.tensor.transpose(ps[:, 4, b * P:(b + 1) * P], rs_rep[:, b, :], ident)
                last.then_inc(s_rt, 1)

            def l0_scores(h, head):
                if h >= 2:
                    pe.wait_ge(s_zs, head - 1)
                if h == 0:
                    pe.wait_ge(post_done, 7 + 3 * (head // 4))
                b = 6 + h % 2
                mm(ps[:, b, 0:P], qT[:, h, 0:P], kT[:, h, 0:P], True, True)
                mm(ps[:, b, P:TRI], qT[:, h, P:T], kT[:, h, :], True, True).then_inc(s_sc, 1)

            def l0_pT(n):
                if n % 2 == 0:
                    pe.wait_ge(s_pn, n + 2)
                else:
                    pe.wait_ge(s_pc, n)
                for i in range(2):
                    for c in range(3):
                        last = nc.tensor.transpose(ps[:, 6 + i, c * P:(c + 1) * P],
                                                   zs[:, 2 * (n % 2) + i, c * P:(c + 1) * P], ident)
                last.then_inc(s_pT, 1)

            def values(b, w):
                for i in range(2):
                    vh = slice((2 * b + i) * P, (2 * b + i + 1) * P)
                    mm(ps[:, 6 + b, i * T:(i + 1) * T], v_sb[:, 0, vh], w[:, i, 0:T], i == 0, False)
                    last = mm(ps[:, 6 + b, i * T + P:(i + 1) * T], v_sb[:, 1, vh], w[:, i, T:TRI], False, True)
                last.then_inc(s_o, 1)

            def l0_values(n, b):
                pe.wait_ge(s_pc, n - n % 2 + 2)
                values(b, tmp[:, 2 * b:2 * b + 2, :])

            def l0_extras(grp):
                e = {2 + h: [lambda h=h: l0_scores(h, 4 * grp + h)] for h in range(4)}
                e.update({13: [lambda: l0_pT(2 * grp)], 14: [lambda: l0_pT(2 * grp + 1)],
                          15: [lambda: l0_values(2 * grp, 0)], 16: [lambda: l0_values(2 * grp + 1, 1)]})
                return e

            def l1_scores(h, grp):
                if h >= 2:
                    pe.wait_ge(s_zs, 4 * grp + (L0_HEADS + h - 1))
                if h == 0:
                    pe.wait_ge(post_done, 3 * grp + (U_IN1 + 3))
                    pe.wait_ge(s_olo, 2 * grp + 4)
                b = 6 + h % 2
                mm(ps[:, b, 0:T], kT[:, h, 0:P], qT[:, h, :], True, True)
                mm(ps[:, b, T:TRI], kT[:, h, P:T], qT[:, h, P:T], True, True).then_inc(s_sc, 1)

            def l1_suffix(b, grp):
                pe.wait_ge(s_splo, 2 * grp + (b + 1))
                pe.wait_ge(s_sums, 1)
                pe.wait_ge(s_zs, 4 * grp + (L0_HEADS + 4))
                if b == 1:
                    pe.wait_ge(s_olo, 2 * grp + 5)
                early = ps[:, 6, :]
                early_q1 = early.rearrange("p (h t) -> p h t", h=2)[:, :, P:T]
                late = ps[:, 7, 0:T]
                suffix_r, ones_r = sum_mats[:, 0:P], sum_mats[:, P:2 * P]
                for z, first in ((soft_hi, True), (soft_lo, False)):
                    mm(early, suffix_r, z[:, :, 0:T], first, False)
                    mm(early_q1, ones_r, z[:, :, T:TRI], False, not first)
                    last = mm(late, suffix_r, z[:, :, T:TRI], first, not first)
                last.then_inc(s_S, 1)

            def l1_values(b, grp):
                pe.wait_ge(s_a, 2 * grp + (b + 1))
                values(b, zs[:, 2 * b:2 * b + 2, :])

            def l1_extras(grp):
                e = {2 + h: [lambda h=h: l1_scores(h, grp)] for h in range(4)}
                e.update({8: [lambda: l1_suffix(0, grp)], 12: [lambda: l1_values(0, grp)],
                          13: [lambda: l1_suffix(1, grp)], 17: [lambda: l1_values(1, grp)]})
                return e

            def qkv_group(u, extras, fresh=None):
                for i, tick in enumerate((tick_features, tick_features, tick_tokens)):
                    unit(u + i, tick, i, fresh=fresh if i == 0 else None,
                         extras={t - 8 * i: f for t, f in extras.items() if 8 * i <= t < 8 * i + 8})

            def out_phase(u0, extras, ready):
                for t, (u, s) in enumerate(OUT_ORDER):
                    for f in extras.get(t, []):
                        f()
                    if s == 0:
                        pe.wait_ge(post_done, u0 + (1 if u == 3 else 0 if u == 2 else -1))
                    if t < 6 or t in (18, 19):
                        for semaphore, value in ready(s):
                            pe.wait_ge(semaphore, value)
                    if t == 28:
                        closing_ticks(OUT_BUF[u], u0 + 3)
                        break
                    tick_tokens(OUT_BUF[u], s, t % RING, hid_hi, hid_lo, 8 * u0 + t + 1)

            def ffn(u0, k):
                def up(g):
                    with pe.Fori(0, 2) as jj:
                        for par in range(2):
                            unit(u0 + 8 * g + 2 * jj + par, tick_features, par)

                def down_pairs(g):
                    with pe.Fori(0, 2) as jj:
                        for par in range(2):
                            down_unit(g, jj, par)

                def down_unit(g, jj, par, closing=False):
                    def hidden_ready(s):
                        if s % 2 == 0:
                            pe.wait_ge(post_done, u0 + 8 * g + (s // 2 + 1))
                    unit(u0 + 8 * g + 4 + 2 * jj + par, tick_tokens, par, hid_hi, hid_lo,
                         before=hidden_ready, closing=closing)

                unit(u0, tick_features, 0, fresh=k)
                for j in range(1, 4):
                    unit(u0 + j, tick_features, j % 2)
                down_pairs(0)
                with pe.Fori(1, FGROUPS - 1) as g:
                    up(g)
                    down_pairs(g)
                up(FGROUPS - 1)
                for j in range(4):
                    down_unit(FGROUPS - 1, j // 2, j % 2, closing=j == 3)

            pe.wait_ge(s_warm, 1)
            for _ in range(WARM_UP):
                mm(ps[:, 1, 0:T], rs_bc[:, 0:P], rs_bc[:, :], True, True)

            pe.wait_ge(s_id, 16)
            pe.wait_ge(s_row0, 16)
            nc.tensor.transpose(ps[:, 0, 0:KT], gain_rows[0:KT], ident[0:KT, 0:KT]).then_inc(s_prepT, 1)

            def small_parts():
                pe.wait_ge(s_rows, 48)
                nc.tensor.transpose(ps[:, 5, 0:4 * KT], gain_rows, ident[0:4 * KT, 0:4 * KT]).then_inc(s_prepT, 1)
                pe.wait_ge(s_tril, 1)
                for g in range(GROUPS):
                    last = nc.tensor.transpose(ps[:, 6 + g // 4, (g % 4) * P:(g % 4 + 1) * P], sgu_nat[:, g, :], ident)
                    if g % 4 == 3:
                        last.then_inc(s_prepT, 1)

            def mix(m):
                if m == 0:
                    pe.wait_ge(s_prep, 3)
                    pe.wait_ge(s_ln, 4)
                if m >= 2:
                    pe.wait_ge(s_sgt, m - 1)
                for i in range(2):
                    g = 2 * m + i
                    for c in range(TB):
                        last = mm(ps[:, 6 + m % 2, i * T + c * P:i * T + (c + 1) * P],
                                  va_n[:, c, g * P:(g + 1) * P], sgu_wT[:, g, :], True, True)
                last.then_inc(s_mix, 1)

            pe.wait_ge(s_prep, 1)
            unit(0, tick_tokens, 0, fresh=0)
            unit(1, tick_tokens, 1, extras={2: [lambda: transpose_scales(0)], 5: [small_parts]})
            unit(2, tick_features, 0)
            unit(3, tick_features, 1)
            qkv_group(4, {1 + m: [lambda m=m: mix(m)] for m in range(4)})
            qkv_group(7, l0_extras(0))

            def ready0(s):
                if s < 4:
                    return [(s_glo, s + 1)]
                return [(s_olo, s - 3)]
            out_phase(U_OUT0, l0_extras(1), ready0)
            transposes(1, U_FFN0)
            ffn(U_FFN0, 1)

            transposes(2, U_IN1)
            qkv_group(U_IN1, {}, fresh=2)
            with pe.Fori(1, L1_GROUPS) as g:
                qkv_group(U_IN1 + 3 * g, l1_extras(g - 1))
            out_phase(U_OUT1, l1_extras(L1_GROUPS - 1), lambda s: [(s_olo, 4 + s + 1)])
            transposes(3, U_FFN1)
            ffn(U_FFN1, 3)


_INS = ['x', 'norm_pre_mix', 'norm_post_mix', 'norm_pre_ffn', 'norm_post_ffn', 'ab_w_in', 'sgu_ln_g', 'sgu_ln_b',
        'sgu_w', 'sgu_b', 'ab_w_out', 'sb_w_in', 'sb_w_out', 'ffn_w1', 'ffn_w2']
_OUT = ((1, T, D), 'float32')


def kernel(**inputs):
    import numpy as _np
    import concourse.bacc as _bacc
    from concourse import mybir as _mybir
    from concourse.bass_utils import run_bass_kernel_spmd as _run

    nc = _bacc.Bacc("TRN2", target_bir_lowering=False, num_devices=1)
    arrays, args = {}, []
    for name in _INS:
        arrays[f"in_{name}_dram"] = _np.ascontiguousarray(inputs[name])
    arrays["shape_constants_dram"] = shape_constants()
    for name, a in arrays.items():
        args.append(nc.dram_tensor(name, a.shape, _mybir.dt.from_np(a.dtype), kind="ExternalInput").ap())
    args.append(nc.dram_tensor("out_dram", _OUT[0], _mybir.dt.from_np(_np.dtype(_OUT[1])), kind="ExternalOutput").ap())
    trunk_kernel(nc, *args)
    r = _run(nc, [arrays], core_ids=[0])
    return r.results[0]["out_dram"]
```
